# Optimizing a Trainium2 kernel written in Bass

```python
import math
import jax, jax.numpy as jnp
from jax import lax
import numpy as np

D_MODEL = 1024
BATCH = 1
SEQ = 256
DEPTH = 2

BLOCK_Q = 128
EPS = 1e-6
MLA_HEADS = 6
MLA_Q_LORA = 384
MLA_KV_LORA = 256
MLA_NOPE = 64
MLA_ROPE = 32
MLA_V = 64
ROPE_THETA = 10000.0
DSA_HEADS = 5
DSA_DIM = 64
IDX_HEADS = 8
IDX_DIM = 64
DSA_TOPK = 256
SB_HEADS = 5
SB_DIM = 64
REL_BUCKETS = 32
REL_MAX_DIST = 128
D_FF = -(-8 * D_MODEL // (3 * 256)) * 256
PLE_DIM = 256

MIX_WIDTH = MLA_HEADS * MLA_V + DSA_HEADS * DSA_DIM + SB_HEADS * SB_DIM
IN_SPLITS = (MLA_Q_LORA, MLA_KV_LORA, MLA_ROPE,
             DSA_HEADS * DSA_DIM, DSA_DIM, DSA_DIM,
             IDX_HEADS * IDX_DIM, IDX_DIM, IDX_HEADS,
             SB_HEADS * SB_DIM, SB_HEADS * SB_DIM, SB_HEADS * SB_DIM)
D_IN = sum(IN_SPLITS)


def rms_norm(x, g):
    xf = x.astype(jnp.float32)
    y = xf * lax.rsqrt(jnp.mean(xf * xf, axis=-1, keepdims=True) + EPS)
    return (y * g.astype(jnp.float32)).astype(x.dtype)

def apply_rope(x, pos):
    half = x.shape[-1] // 2
    inv = ROPE_THETA ** (-jnp.arange(half, dtype=jnp.float32) / half)
    ang = pos.astype(jnp.float32)[:, None] * inv[None, :]
    cos = jnp.cos(ang)[None, :, None, :].astype(x.dtype)
    sin = jnp.sin(ang)[None, :, None, :].astype(x.dtype)
    x1, x2 = x[..., :half], x[..., half:]
    return jnp.concatenate([x1 * cos - x2 * sin, x1 * sin + x2 * cos], axis=-1)

def t5_bucket(dist):
    max_exact = REL_BUCKETS // 2
    d = jnp.maximum(dist, 1).astype(jnp.float32)
    large = max_exact + (jnp.log(d / max_exact) / math.log(REL_MAX_DIST / max_exact)
                         * (REL_BUCKETS - max_exact)).astype(jnp.int32)
    large = jnp.minimum(large, REL_BUCKETS - 1)
    return jnp.where(dist < max_exact, dist, large)

def mixer_block(q0, pos, mla_q, mla_k, mla_v, dsa_q, dsa_k, dsa_v,
                idx_q, idx_k, idx_w, sb_q, sb_k, sb_v, rel_bias, topk):
    B = mla_q.shape[0]
    sl = lambda a: lax.dynamic_slice_in_dim(a, q0, BLOCK_Q, axis=1)
    qpos = q0 + jnp.arange(BLOCK_Q, dtype=jnp.int32)
    causal = pos[None, :] <= qpos[:, None]
    strict = pos[None, :] < qpos[:, None]

    s = jnp.einsum('bqhd,bkhd->bhqk', sl(mla_q), mla_k).astype(jnp.float32) * (MLA_NOPE + MLA_ROPE) ** -0.5
    s = jnp.where(causal[None, None], s, -jnp.inf)
    pr = jax.nn.softmax(s, axis=-1).astype(mla_v.dtype)
    o_mla = jnp.einsum('bhqk,bkhd->bqhd', pr, mla_v).reshape(B, BLOCK_Q, MLA_HEADS * MLA_V)

    ilog = jnp.einsum('bqhd,bkd->bqhk', sl(idx_q), idx_k) * IDX_DIM ** -0.5
    isc = jnp.einsum('bqhk,bqh->bqk', jax.nn.relu(ilog), sl(idx_w)).astype(jnp.float32)
    isc = jnp.where(causal[None], isc, -jnp.inf)
    _, sel = lax.top_k(isc, topk)
    valid = sel <= qpos[None, :, None]
    gather = jax.vmap(lambda a, i: a[i])
    kg = gather(dsa_k, sel)
    vg = gather(dsa_v, sel)
    bias = rel_bias[t5_bucket(jnp.maximum(qpos[None, :, None] - sel, 0))]
    a = (jnp.einsum('bqhd,bqjd->bhqj', sl(dsa_q), kg).astype(jnp.float32) * DSA_DIM ** -0.5
         + jnp.transpose(bias, (0, 3, 1, 2)).astype(jnp.float32))
    a = jnp.where(valid[:, None], a, -jnp.inf)
    pa = jax.nn.softmax(a, axis=-1).astype(vg.dtype)
    o_dsa = jnp.einsum('bhqj,bqjd->bqhd', pa, vg).reshape(B, BLOCK_Q, DSA_HEADS * DSA_DIM)

    z = jnp.einsum('bqhd,bkhd->bhqk', sl(sb_q), sb_k).astype(jnp.float32) * SB_DIM ** -0.5
    m = strict[None, None]
    l1m = jnp.where(m, jax.nn.log_sigmoid(-z), 0.0)
    suffix = lax.cumsum(l1m, axis=3, reverse=True) - l1m
    w = jnp.where(m, jnp.exp(jax.nn.log_sigmoid(z) + suffix), 0.0).astype(sb_v.dtype)
    o_sb = jnp.einsum('bhqk,bkhd->bqhd', w, sb_v).reshape(B, BLOCK_Q, SB_HEADS * SB_DIM)

    return jnp.concatenate([o_mla, o_dsa, o_sb], axis=-1)

def first_inputs(seed: int = 0) -> dict:
    key = jax.random.key(seed)
    ks = jax.random.split(key, 18)
    f32 = jnp.float32
    nrm = lambda k, shape, scale: jax.random.normal(k, shape, f32) * scale
    gain = lambda k, shape: 1.0 + 0.05 * jax.random.normal(k, shape, f32)
    return {
        "x": nrm(ks[0], (BATCH, SEQ, D_MODEL), 1.0),
        "p": nrm(ks[1], (DEPTH, BATCH, SEQ, PLE_DIM), 1.0),
        "w_in": nrm(ks[2], (DEPTH, D_MODEL, D_IN), D_MODEL ** -0.5),
        "attn_norm": gain(ks[3], (DEPTH, D_MODEL)),
        "mla_q_norm": gain(ks[4], (DEPTH, MLA_Q_LORA)),
        "mla_w_uq": nrm(ks[5], (DEPTH, MLA_Q_LORA, MLA_HEADS * (MLA_NOPE + MLA_ROPE)), MLA_Q_LORA ** -0.5),
        "mla_kv_norm": gain(ks[6], (DEPTH, MLA_KV_LORA)),
        "mla_w_ukv": nrm(ks[7], (DEPTH, MLA_KV_LORA, MLA_HEADS * (MLA_NOPE + MLA_V)), MLA_KV_LORA ** -0.5),
        "rel_bias": nrm(ks[8], (REL_BUCKETS, DSA_HEADS), 0.5),
        "w_o": nrm(ks[9], (DEPTH, MIX_WIDTH, D_MODEL), MIX_WIDTH ** -0.5),
        "ffn_norm": gain(ks[10], (DEPTH, D_MODEL)),
        "w_gate": nrm(ks[11], (DEPTH, D_MODEL, D_FF), D_MODEL ** -0.5),
        "w_up": nrm(ks[12], (DEPTH, D_MODEL, D_FF), D_MODEL ** -0.5),
        "w_down": nrm(ks[13], (DEPTH, D_FF, D_MODEL), D_FF ** -0.5),
        "ple_norm": gain(ks[14], (DEPTH, D_MODEL)),
        "w_ple_gate": nrm(ks[15], (DEPTH, D_MODEL, D_MODEL), D_MODEL ** -0.5),
        "w_ple_proj": nrm(ks[16], (DEPTH, PLE_DIM, D_MODEL), PLE_DIM ** -0.5),
        "final_norm": gain(ks[17], (D_MODEL,)),
    }

def first_block(x, p, w_in, attn_norm, mla_q_norm, mla_w_uq, mla_kv_norm, mla_w_ukv,
              rel_bias, w_o, ffn_norm, w_gate, w_up, w_down, ple_norm, w_ple_gate,
              w_ple_proj, final_norm):
    B, S, _ = x.shape
    n_blk = S // BLOCK_Q
    topk = min(DSA_TOPK, S // 4)
    pos = jnp.arange(S, dtype=jnp.int32)
    offsets = [int(o) for o in np.cumsum(IN_SPLITS)[:-1]]
    starts = jnp.arange(n_blk, dtype=jnp.int32) * BLOCK_Q
    h = x
    for i in range(DEPTH):
        hn = rms_norm(h, attn_norm[i])
        proj = hn @ w_in[i]
        (c_q, c_kv, k_rope, dq, dk, dv, iq, ik, iw, sq, sk, sv) = jnp.split(proj, offsets, axis=-1)

        q = (rms_norm(c_q, mla_q_norm[i]) @ mla_w_uq[i]).reshape(B, S, MLA_HEADS, MLA_NOPE + MLA_ROPE)
        q = jnp.concatenate([q[..., :MLA_NOPE], apply_rope(q[..., MLA_NOPE:], pos)], axis=-1)
        kv = (rms_norm(c_kv, mla_kv_norm[i]) @ mla_w_ukv[i]).reshape(B, S, MLA_HEADS, MLA_NOPE + MLA_V)
        kr = apply_rope(k_rope[:, :, None, :], pos)
        mla_k = jnp.concatenate([kv[..., :MLA_NOPE],
                                 jnp.broadcast_to(kr, (B, S, MLA_HEADS, MLA_ROPE))], axis=-1)
        mla_v = kv[..., MLA_NOPE:]

        dsa_q = dq.reshape(B, S, DSA_HEADS, DSA_DIM)
        idx_q = iq.reshape(B, S, IDX_HEADS, IDX_DIM)
        idx_w = iw * IDX_HEADS ** -0.5

        sb_q = sq.reshape(B, S, SB_HEADS, SB_DIM)
        sb_k = sk.reshape(B, S, SB_HEADS, SB_DIM)
        sb_v = sv.reshape(B, S, SB_HEADS, SB_DIM)

        blocks = lax.map(lambda q0: mixer_block(q0, pos, q, mla_k, mla_v, dsa_q, dk, dv,
                                                idx_q, ik, idx_w, sb_q, sb_k, sb_v,
                                                rel_bias, topk), starts)
        mix = jnp.transpose(blocks, (1, 0, 2, 3)).reshape(B, S, MIX_WIDTH)
        h = h + mix @ w_o[i]

        hf = rms_norm(h, ffn_norm[i])
        h = h + (jax.nn.silu(hf @ w_gate[i]) * (hf @ w_up[i])) @ w_down[i]

        g = jax.nn.sigmoid(rms_norm(h, ple_norm[i]) @ w_ple_gate[i])
        h = h + g * (p[i] @ w_ple_proj[i])
    return rms_norm(h, final_norm)


N_A = DEPTH // 2
N_B = DEPTH - N_A
HEAD_DIM = 64
MIX_WIDTH_2 = D_MODEL
MEM_HEADS = 4
MEM_WIDTH = MEM_HEADS * HEAD_DIM
MEM_LEN = 256
CONV_CH = MIX_WIDTH_2 - MEM_WIDTH
CONV_K = 3
NSA_HEADS = CONV_CH // HEAD_DIM
NSA_KV_GROUPS = 2
NSA_HPG = NSA_HEADS // NSA_KV_GROUPS
N_BRANCH = 3
NSA_Q_WIDTH = NSA_HEADS * HEAD_DIM
NSA_GATE_WIDTH = NSA_HEADS * N_BRANCH
CMP_LEN = 32
CMP_STRIDE = 16
CMP_HIDDEN = 256
SEL_BLOCK = 64
SEL_TOPK = 16
N_LOCAL_SEL = 2
WINDOW = 512
Q_BLOCK = 128
REL_MAX_DIST_2 = 1024
FF_DIM = 4 * D_MODEL
NEG = -1e30
FORCE_SCORE = 1e4


def rmsnorm(x, g):
    xf = x.astype(jnp.float32)
    y = xf * lax.rsqrt(jnp.mean(xf * xf, axis=-1, keepdims=True) + EPS)
    return (y * g.astype(jnp.float32)).astype(x.dtype)

def rel_bucket(dist):
    n = jnp.maximum(dist, 0)
    max_exact = REL_BUCKETS // 2
    nf = jnp.maximum(n, 1).astype(jnp.float32)
    large = max_exact + (jnp.log(nf / max_exact) / math.log(REL_MAX_DIST_2 / max_exact)
                         * (REL_BUCKETS - max_exact)).astype(jnp.int32)
    large = jnp.minimum(large, REL_BUCKETS - 1)
    return jnp.where(n < max_exact, n, large)

def masked_softmax(logits, mask):
    p = jax.nn.softmax(jnp.where(mask, logits, NEG), axis=-1)
    return jnp.where(mask, p, 0.0)

def selection_overlap(n_cmp, n_sel):
    c0 = np.arange(n_cmp)[:, None] * CMP_STRIDE
    s0 = np.arange(n_sel)[None, :] * SEL_BLOCK
    ov = np.minimum(c0 + CMP_LEN, s0 + SEL_BLOCK) - np.maximum(c0, s0)
    return np.clip(ov, 0, None).astype(np.float32) / CMP_LEN

def short_conv_mixer(z, conv_w):
    gate_b, gate_c, u = jnp.split(z, 3, axis=-1)
    v = gate_c * u
    y = lax.conv_general_dilated(
        v, conv_w[:, None, :].astype(v.dtype), window_strides=(1,),
        padding=[(CONV_K - 1, 0)], dimension_numbers=('NWC', 'WIO', 'NWC'),
        feature_group_count=CONV_CH)
    return gate_b * y

def memory_attention(q_raw, mem_k, mem_v, q_gain):
    b, s, _ = q_raw.shape
    q = rmsnorm(q_raw.reshape(b, s, MEM_HEADS, HEAD_DIM), q_gain) * (HEAD_DIM ** -0.5)
    lg = jnp.einsum('bshd,bmhd->bhsm', q, mem_k).astype(jnp.float32)
    p = jax.nn.softmax(lg, axis=-1).astype(mem_v.dtype)
    return jnp.einsum('bhsm,bmhd->bshd', p, mem_v).reshape(b, s, MEM_WIDTH)

def compress(u, pos, w1, w2):
    b, s, g, d = u.shape
    ch = u.reshape(b, s // CMP_STRIDE, CMP_STRIDE, g, d)
    blk = jnp.concatenate([ch[:, :-1], ch[:, 1:]], axis=2) + pos[:, None, :]
    flat = blk.transpose(0, 1, 3, 2, 4).reshape(b, -1, g, CMP_LEN * d)
    return jax.nn.gelu(flat @ w1) @ w2

def build_shared_kv(x, kv_norm, w_kv_shared, k_gain, cmp_pos, cmp_w1, cmp_w2):
    b, s, _ = x.shape
    h = rmsnorm(x, kv_norm)
    kv = (h @ w_kv_shared).reshape(b, s, 6, NSA_KV_GROUPS, HEAD_DIM)
    kc = rmsnorm(compress(kv[:, :, 0], cmp_pos[0], cmp_w1[0], cmp_w2[0]), k_gain[0])
    vc = compress(kv[:, :, 1], cmp_pos[1], cmp_w1[1], cmp_w2[1])
    n_sel = s // SEL_BLOCK
    def to_blocks(u):
        return u.reshape(b, n_sel, SEL_BLOCK, NSA_KV_GROUPS, HEAD_DIM).transpose(0, 3, 1, 2, 4)
    ks = to_blocks(rmsnorm(kv[:, :, 2], k_gain[1]))
    vs = to_blocks(kv[:, :, 3])
    def pad_front(u):
        return jnp.pad(u, ((0, 0), (WINDOW, 0), (0, 0), (0, 0)))
    kw = pad_front(rmsnorm(kv[:, :, 4], k_gain[2]))
    vw = pad_front(kv[:, :, 5])
    return (kc, vc, ks, vs, kw, vw)

def nsa_mixer(q_raw, gate_logits, q_gain, kc, vc, ks, vs, kw, vw, rel_bias):
    b, s, _ = q_raw.shape
    G, Hg, hd = NSA_KV_GROUPS, NSA_HPG, HEAD_DIM
    q = rmsnorm(q_raw.reshape(b, s, G, Hg, hd), q_gain) * (hd ** -0.5)
    gates = jax.nn.sigmoid(gate_logits.reshape(b, s, G, Hg, N_BRANCH))
    n_cmp = kc.shape[1]
    n_sel = ks.shape[2]
    topk = min(SEL_TOPK, n_sel)
    overlap = jnp.asarray(selection_overlap(n_cmp, n_sel), dtype=jnp.float32)
    cmp_end = jnp.arange(n_cmp) * CMP_STRIDE + CMP_LEN - 1
    sel_idx = jnp.arange(n_sel)
    table = rel_bias.astype(jnp.float32)
    table_g = table.reshape(REL_BUCKETS, G, Hg).transpose(1, 0, 2)
    bi = jnp.arange(b)[:, None, None, None]
    gi = jnp.arange(G)[None, :, None, None]
    kw_len = WINDOW + Q_BLOCK

    def block(i):
        s0 = i * Q_BLOCK
        tq = s0 + jnp.arange(Q_BLOCK)
        qb = lax.dynamic_slice_in_dim(q, s0, Q_BLOCK, axis=1)
        gb = lax.dynamic_slice_in_dim(gates, s0, Q_BLOCK, axis=1)
        d_c = tq[:, None] - cmp_end[None, :]
        bias_c = table[rel_bucket(d_c)].reshape(Q_BLOCK, n_cmp, G, Hg).transpose(2, 3, 0, 1)
        lg = jnp.einsum('bqghd,bcgd->bghqc', qb, kc).astype(jnp.float32) + bias_c
        p_c = masked_softmax(lg, d_c >= 0)
        o_c = jnp.einsum('bghqc,bcgd->bqghd', p_c.astype(vc.dtype), vc)
        imp = jnp.einsum('bghqc,cj->bgqj', p_c, overlap)
        back = (tq // SEL_BLOCK)[:, None] - sel_idx[None, :]
        forced = (sel_idx[None, :] == 0) | ((back >= 0) & (back < N_LOCAL_SEL))
        score = jnp.where(back >= 0, jnp.where(forced, FORCE_SCORE, imp), NEG)
        _, idx = lax.top_k(score, topk)
        k_sel = ks[bi, gi, idx].reshape(b, G, Q_BLOCK, topk * SEL_BLOCK, hd)
        v_sel = vs[bi, gi, idx].reshape(b, G, Q_BLOCK, topk * SEL_BLOCK, hd)
        pos_s = (idx[..., None] * SEL_BLOCK + jnp.arange(SEL_BLOCK)).reshape(b, G, Q_BLOCK, topk * SEL_BLOCK)
        d_s = tq[None, None, :, None] - pos_s
        bias_s = table_g[gi, rel_bucket(d_s)].transpose(0, 1, 4, 2, 3)
        lg = jnp.einsum('bqghd,bgqkd->bghqk', qb, k_sel).astype(jnp.float32) + bias_s
        p_s = masked_softmax(lg, (d_s >= 0)[:, :, None])
        o_s = jnp.einsum('bghqk,bgqkd->bqghd', p_s.astype(v_sel.dtype), v_sel)
        k_w = lax.dynamic_slice_in_dim(kw, s0, kw_len, axis=1)
        v_w = lax.dynamic_slice_in_dim(vw, s0, kw_len, axis=1)
        pos_w = s0 - WINDOW + jnp.arange(kw_len)
        d_w = tq[:, None] - pos_w[None, :]
        mask_w = (d_w >= 0) & (d_w < WINDOW) & (pos_w[None, :] >= 0)
        bias_w = table[rel_bucket(d_w)].reshape(Q_BLOCK, kw_len, G, Hg).transpose(2, 3, 0, 1)
        lg = jnp.einsum('bqghd,bkgd->bghqk', qb, k_w).astype(jnp.float32) + bias_w
        p_w = masked_softmax(lg, mask_w)
        o_w = jnp.einsum('bghqk,bkgd->bqghd', p_w.astype(v_w.dtype), v_w)
        return gb[..., 0:1] * o_c + gb[..., 1:2] * o_s + gb[..., 2:3] * o_w

    out = lax.map(block, jnp.arange(s // Q_BLOCK))
    return jnp.moveaxis(out, 0, 1).reshape(b, s, NSA_Q_WIDTH)

def second_inputs(seed: int = 0) -> dict:
    key = jax.random.key(seed)
    ks = jax.random.split(key, 22)
    def nrm(k, shape, scale):
        return jax.random.normal(k, shape, jnp.float32) * scale
    def gain(k, shape):
        return 1.0 + 0.1 * jax.random.normal(k, shape, jnp.float32)
    a_in = 3 * CONV_CH + MEM_WIDTH
    b_in = NSA_Q_WIDTH + NSA_GATE_WIDTH + MEM_WIDTH
    return {
        "x": nrm(ks[0], (BATCH, SEQ, D_MODEL), 1.0),
        "mem": nrm(ks[1], (BATCH, MEM_LEN, D_MODEL), 1.0),
        "mix_norm": gain(ks[2], (DEPTH, D_MODEL)),
        "a_w_in": nrm(ks[3], (N_A, D_MODEL, a_in), D_MODEL ** -0.5),
        "a_conv_w": nrm(ks[4], (N_A, CONV_K, CONV_CH), CONV_K ** -0.5),
        "b_w_in": nrm(ks[5], (N_B, D_MODEL, b_in), D_MODEL ** -0.5),
        "b_q_gain": gain(ks[6], (N_B, HEAD_DIM)),
        "kv_norm": gain(ks[7], (D_MODEL,)),
        "w_kv_shared": nrm(ks[8], (D_MODEL, 6 * NSA_KV_GROUPS * HEAD_DIM), D_MODEL ** -0.5),
        "k_gain": gain(ks[9], (N_BRANCH, HEAD_DIM)),
        "cmp_pos": nrm(ks[10], (2, CMP_LEN, HEAD_DIM), 0.1),
        "cmp_w1": nrm(ks[11], (2, CMP_LEN * HEAD_DIM, CMP_HIDDEN), (CMP_LEN * HEAD_DIM) ** -0.5),
        "cmp_w2": nrm(ks[12], (2, CMP_HIDDEN, HEAD_DIM), CMP_HIDDEN ** -0.5),
        "rel_bias": nrm(ks[13], (REL_BUCKETS, NSA_HEADS), 0.5),
        "mem_norm": gain(ks[14], (D_MODEL,)),
        "mem_w_kv": nrm(ks[15], (DEPTH, D_MODEL, 2 * MEM_WIDTH), D_MODEL ** -0.5),
        "mem_q_gain": gain(ks[16], (DEPTH, HEAD_DIM)),
        "mem_k_gain": gain(ks[17], (DEPTH, HEAD_DIM)),
        "w_out": nrm(ks[18], (DEPTH, MIX_WIDTH_2, D_MODEL), MIX_WIDTH_2 ** -0.5),
        "mlp_norm": gain(ks[19], (DEPTH, D_MODEL)),
        "w_up": nrm(ks[20], (DEPTH, D_MODEL, FF_DIM), D_MODEL ** -0.5),
        "w_down": nrm(ks[21], (DEPTH, FF_DIM, D_MODEL), FF_DIM ** -0.5),
    }

def second_block(x, mem, mix_norm, a_w_in, a_conv_w, b_w_in, b_q_gain, kv_norm, w_kv_shared,
              k_gain, cmp_pos, cmp_w1, cmp_w2, rel_bias, mem_norm, mem_w_kv, mem_q_gain,
              mem_k_gain, w_out, mlp_norm, w_up, w_down):
    b, m, _ = mem.shape
    mem_h = rmsnorm(mem, mem_norm)
    shared = None
    for layer in range(DEPTH):
        h = rmsnorm(x, mix_norm[layer])
        mkv = (mem_h @ mem_w_kv[layer]).reshape(b, m, 2, MEM_HEADS, HEAD_DIM)
        mem_k = rmsnorm(mkv[:, :, 0], mem_k_gain[layer])
        mem_v = mkv[:, :, 1]
        if layer < N_A:
            z = h @ a_w_in[layer]
            y_tok = short_conv_mixer(z[..., :3 * CONV_CH], a_conv_w[layer])
            q_mem = z[..., 3 * CONV_CH:]
        else:
            j = layer - N_A
            z = h @ b_w_in[j]
            y_tok = nsa_mixer(z[..., :NSA_Q_WIDTH],
                              z[..., NSA_Q_WIDTH:NSA_Q_WIDTH + NSA_GATE_WIDTH],
                              b_q_gain[j], *shared, rel_bias)
            q_mem = z[..., NSA_Q_WIDTH + NSA_GATE_WIDTH:]
        y_mem = memory_attention(q_mem, mem_k, mem_v, mem_q_gain[layer])
        x = x + jnp.concatenate([y_tok, y_mem], axis=-1) @ w_out[layer]
        hm = rmsnorm(x, mlp_norm[layer])
        x = x + jnp.square(jax.nn.relu(hm @ w_up[layer])) @ w_down[layer]
        if layer == N_A - 1:
            shared = build_shared_kv(x, kv_norm, w_kv_shared, k_gain, cmp_pos, cmp_w1, cmp_w2)
    return x


def setup_inputs(seed=0):
    out = dict(first_inputs(seed))
    for name, value in second_inputs(seed + 1).items():
        if name != "x":
            out[name + "_2"] = value
    return out


def reference(
    x, p, w_in, attn_norm, mla_q_norm, mla_w_uq, mla_kv_norm, mla_w_ukv, rel_bias, w_o,
    ffn_norm, w_gate, w_up, w_down, ple_norm, w_ple_gate, w_ple_proj, final_norm, mem_2,
    mix_norm_2, a_w_in_2, a_conv_w_2, b_w_in_2, b_q_gain_2, kv_norm_2, w_kv_shared_2, k_gain_2,
    cmp_pos_2, cmp_w1_2, cmp_w2_2, rel_bias_2, mem_norm_2, mem_w_kv_2, mem_q_gain_2,
    mem_k_gain_2, w_out_2, mlp_norm_2, w_up_2, w_down_2,
):
    x = first_block(
        x, p, w_in, attn_norm, mla_q_norm, mla_w_uq, mla_kv_norm, mla_w_ukv, rel_bias, w_o,
        ffn_norm, w_gate, w_up, w_down, ple_norm, w_ple_gate, w_ple_proj, final_norm,
    )
    return second_block(
        x, mem_2, mix_norm_2, a_w_in_2, a_conv_w_2, b_w_in_2, b_q_gain_2, kv_norm_2,
        w_kv_shared_2, k_gain_2, cmp_pos_2, cmp_w1_2, cmp_w2_2, rel_bias_2, mem_norm_2,
        mem_w_kv_2, mem_q_gain_2, mem_k_gain_2, w_out_2, mlp_norm_2, w_up_2, w_down_2,
    )


_drawn_inputs = setup_inputs


def setup_inputs(seed=0):
    import zlib

    import numpy as np

    out = dict(_drawn_inputs(seed))
    spreads = {}
    factors = {'mla_q_norm': 4.439,
     'mla_kv_norm': 2.727,
     'ple_norm': 2.896,
     'b_q_gain_2': 7.959,
     'kv_norm_2': 3.014,
     'k_gain_2': 7.137,
     'cmp_pos_2': 3.652,
     'mem_norm_2': 7.323,
     'mem_q_gain_2': 8.0,
     'mem_k_gain_2': 8.0}
    for name, (base, spread) in spreads.items():
        noise = np.random.default_rng([zlib.crc32(name.encode()), seed]).standard_normal(out[name].shape)
        drawn = base * np.exp(spread * noise) if base else spread * noise
        out[name] = __import__('jax').numpy.asarray(drawn.astype(out[name].dtype))
    for name, factor in factors.items():
        out[name] = (out[name] * factor).astype(out[name].dtype)
    return out
```

```python
from contextlib import ExitStack

import numpy as np

import concourse.bass as bass
from concourse import mybir

ALU = mybir.AluOpType
ACT = mybir.ActivationFunctionType
F32 = mybir.dt.float32
F32R = mybir.dt.float32r
AX_X = mybir.AxisListType.X

P = 128
D = 1024
S = 256
NT = S // P
KD = D // P
DEPTH = 2
EPS = 1e-6
NEG = -1e30

MLA_H, MLA_Q, MLA_KV, NOPE, ROPE, VDIM = 6, 384, 256, 64, 32, 64
QK = NOPE + ROPE
DSA_H, IDX_H, SB_H, HD = 5, 8, 5, 64
TOPK = S // 4
FF1 = 2816
PLE = 256
IN_SPLITS = (MLA_Q, MLA_KV, ROPE, DSA_H * HD, HD, HD, IDX_H * HD, HD, IDX_H, SB_H * HD, SB_H * HD, SB_H * HD)
O_CQ, O_CKV, O_KR, O_DQ, O_DK, O_DV, O_IQ, O_IK, O_IW, O_SQ, O_SK, O_SV, D_IN = (
    [0] + [int(v) for v in np.cumsum(IN_SPLITS)])
MIX_DSA = MLA_H * VDIM
MIX_SB = MIX_DSA + DSA_H * HD

CONV = 768
MEM_H = 4
MEM_W = MEM_H * HD
NSA_H = 12
NSA_G = 2
HPG = NSA_H // NSA_G
B_IN = NSA_H * HD + 3 * NSA_H + MEM_W
CMP_LEN, CMP_STRIDE, CMP_HID = 32, 16, 256
A_IN = 3 * CONV + MEM_W
NCMP = S // CMP_STRIDE - 1
FF2 = 4 * D

PW = 2048
RR = 3
RH = 3
BUCKETS = 32
NROWS = DSA_H + 1 + NSA_H
WORK = 15900
TAKEN = -3e38
HEADS1 = SB_H + MLA_H + DSA_H


def sub(name, layer, k0, nk, c0, nc_):
    return (name, layer, k0, nk, c0, nc_)


def wide(name, layer, n):
    out = []
    for c0 in range(0, n, 512):
        w = min(512, n - c0)
        step = 4 if w > 256 else KD
        out += [sub(name, layer, k0, step, c0, w) for k0 in range(0, KD, step)]
    return out


def tall(name, layer, k):
    return [sub(name, layer, k0, 2, 0, D) for k0 in range(0, k, 2)]


def ffn_order(up, down):
    out = list(up[0])
    for c in range(1, len(up)):
        out += up[c] + [down[c - 1]]
    return out + [down[-1]]


def plan():
    pieces, first = [], {}

    def add(stage, items):
        first[stage] = len(pieces)
        pieces.extend(items)

    for l in range(DEPTH):
        add(("w_in", l), wide("w_in", l, D_IN))
        add(("uq", l), [sub("mla_w_uq", l, 0, 3, 0, MLA_H * QK)])
        add(("ukv", l), [sub("mla_w_ukv", l, 0, 2, 0, MLA_H * (NOPE + VDIM))])
        add(("w_o", l), tall("w_o", l, KD))
        add(("ffn1", l), ffn_order([[sub("w_gate", l, 0, KD, c * 256, 256), sub("w_up", l, 0, KD, c * 256, 256)]
                                    for c in range(FF1 // 256)], tall("w_down", l, FF1 // P)))
        add(("ple_gate", l), tall("w_ple_gate", l, KD))
        add(("ple_proj", l), tall("w_ple_proj", l, PLE // P))
    for l in range(DEPTH):
        add(("mem_kv", l), wide("mem_w_kv_2", l, 2 * MEM_W))
    for l in range(DEPTH):
        if l == 0:
            add(("a_in", l), wide("a_w_in_2", 0, A_IN))
        else:
            add(("kv", l), wide("w_kv_shared_2", 0, 6 * NSA_G * HD))
            add(("b_in", l), wide("b_w_in_2", 0, B_IN))
            for which in range(2):
                add(("cmp", which), [sub("cmp_w1_2", which, k0, KD, 0, CMP_HID) for k0 in (0, KD)])
        add(("w_out", l), tall("w_out_2", l, KD))
        add(("ffn2", l), ffn_order([[sub("w_up_2", l, 0, KD, c * 256, 256)] for c in range(FF2 // 256)],
                                   tall("w_down_2", l, FF2 // P)))
    return pieces, first


PIECES, FIRST = plan()


def piece_width(p):
    return PIECES[p][3] * PIECES[p][5]


COLS = {}
_n = 0
for _name, _k in ([(("attn_norm", l), 8) for l in range(2)] + [(("mla_q_norm", l), 3) for l in range(2)]
                  + [(("mla_kv_norm", l), 2) for l in range(2)] + [(("ffn_norm", l), 8) for l in range(2)]
                  + [(("ple_norm", l), 8) for l in range(2)]
                  + [(("mem_norm_2", None), 8), (("kv_norm_2", None), 8)]
                  + [(("mix_norm_2", l), 8) for l in range(2)] + [(("mlp_norm_2", l), 8) for l in range(2)]
                  + [(("mem_k_gain_2", l), 1) for l in range(2)] + [(("mem_q_gain_2", l), 1) for l in range(2)]
                  + [(("k_gain_2", l), 1) for l in range(3)] + [(("b_q_gain_2", 0), 1)]
                  + [(("cmp_pos_2", l), 16) for l in range(2)]
                  + [(("a_conv_w_2", k), 6) for k in range(3)]):
    COLS[_name] = _n
    _n += _k
NCOLS = _n

C_ID, C_FLIP, C_TRI, C_ONES, C_COS, C_SIN, C_SMASK, C_NEGM, C_SEEN, NCONST = [
    int(v) for v in np.cumsum([0, 128, 128, 128, 128, 32, 32, 384, 384, 2])]


def constants():
    c = np.zeros((P, NCONST), np.float32)
    i = np.arange(P)
    c[:, C_ID:C_ID + P] = np.eye(P)
    c[:, C_FLIP:C_FLIP + P] = np.eye(P)[::-1]
    c[:, C_TRI:C_TRI + P] = i[:, None] >= i[None, :]
    c[:, C_ONES:C_ONES + P] = 1.0
    half = ROPE // 2
    inv = np.float32(10000.0) ** (-np.arange(half, dtype=np.float32) / np.float32(half))
    ang = np.arange(S, dtype=np.float32)[:, None] * inv[None, :]
    c[:, C_COS:C_COS + 32] = np.cos(ang).reshape(NT, P, half).transpose(1, 0, 2).reshape(P, 32)
    c[:, C_SIN:C_SIN + 32] = np.sin(ang).reshape(NT, P, half).transpose(1, 0, 2).reshape(P, 32)
    q = np.concatenate([np.arange(S), np.arange(P)])
    valid = q[None, :] > i[:, None]
    c[:, C_SMASK:C_SMASK + 384] = np.where(valid, 0.0, NEG)
    c[:, C_NEGM:C_NEGM + 384] = np.where(valid, -HD ** 0.5, 0.0)
    c[:, C_SEEN] = i >= CMP_LEN - 1
    c[:, C_SEEN + 1] = 1.0
    return c


def gains(name, k):
    return [COLS[name] + j for j in range(k)]


def ffn_places(p, blocks, per_up):
    ups = [p] + [p + per_up + (per_up + 1) * (c - 1) for c in range(1, blocks)]
    downs = [p + per_up * 2 + (per_up + 1) * c for c in range(blocks - 1)] + [p + (per_up + 1) * blocks - 1]
    return ups, downs


def one_hot():
    o = np.zeros((BUCKETS + 1, 2, 512), np.float32)
    for which, far in enumerate((128, 1024)):
        n = np.arange(S)
        big = 16 + (np.log(np.maximum(n, 1).astype(np.float32) / np.float32(16))
                    / np.float32(np.log(far / 16)) * np.float32(16)).astype(np.int32)
        bucket = np.where(n < 16, n, np.minimum(big, 31))
        for j in range(512):
            o[bucket[255 - j] if j <= 255 else BUCKETS, which, j] = 1.0
    return o


def bass_two_blocks(nc, weights, x_in, p_in, cols_in, consts_in, onehot_in, tables_in, final_in, mem_in,
                    w2_in, out):
    ctx = ExitStack()
    with ctx:
        def sb(name, shape, dt=F32):
            return ctx.enter_context(nc.sbuf_tensor(name, shape, dt))

        def sem(name):
            return ctx.enter_context(nc.semaphore(name))

        raw = sb("raw", [P, RR, PW])
        w_hi = sb("w_hi", [P, RH, PW], F32R)
        w_lo = sb("w_lo", [P, RH, PW], F32R)
        h = sb("h", [P, NT, D])
        xs = sb("xs", [P, NT, D])
        xT = sb("xT", [P, 2, KD, S], F32R)
        hT = sb("hT", [P, 2, 5, S], F32R)
        Lb = sb("Lb", [P, 2, 512])
        Pb = sb("Pb", [P, 2, 512])
        PTb = sb("PTb", [P, 2, 512])
        cst = sb("cst", [P, NCONST])
        col = sb("col", [P, NCOLS])
        ss = sb("ss", [P, 4])
        ms = sb("ms", [P, 4])
        expo = sb("expo", [P, 32])
        rstd = sb("rstd", [P, 4])
        nmax = sb("nmax", [P, 2, NT])
        rows = sb("rows", [P, 8, NT])
        rinv = sb("rinv", [P, 4, NT])
        hss = sb("hss", [P, 32])
        hms = sb("hms", [P, 32])
        hrs = sb("hrs", [P, 32])
        pT = sb("pT", [P, PLE // P, S])
        Tdsa = sb("Tdsa", [P, DSA_H + 1, S])
        work = sb("work", [P, WORK])

        PS = [ctx.enter_context(nc.psum_tensor(f"ps{i}", [P, 512], F32)) for i in range(8)]

        R_dram = nc.dram_tensor("distance_rows", (NROWS, 512), F32, kind="Internal")

        ident = cst[:, C_ID:C_ID + P]
        flip = cst[:, C_FLIP:C_FLIP + P]
        tri = cst[:, C_TRI:C_TRI + P]
        ones = cst[:, C_ONES:C_ONES + P]
        cos = cst[:, C_COS:C_COS + 32].rearrange("p (t f) -> p t f", t=NT)
        sin = cst[:, C_SIN:C_SIN + 32].rearrange("p (t f) -> p t f", t=NT)
        smask = cst[:, C_SMASK:C_SMASK + 384]
        negm = cst[:, C_NEGM:C_NEGM + 384]

        def carver(region, size):
            at = [0]

            def take(*shape):
                n = int(np.prod(shape))
                v = region[:, at[0]:at[0] + n]
                at[0] += n
                assert at[0] <= size, (at[0], size)
                if len(shape) == 2:
                    return v.rearrange("p (a b) -> p a b", a=shape[0])
                if len(shape) == 3:
                    return v.rearrange("p (a b c) -> p a b c", a=shape[0], b=shape[1])
                return v
            return take

        take = carver(work, WORK)
        proj = take(NT, D_IN)
        allT = take(15, S)
        kcat = take(NT, MLA_H, QK)
        qT = take(MLA_H, S)
        kT = take(MLA_H, S)
        vmla = take(NT, MLA_H, VDIM)
        isc = take(384)
        selm = take(384)
        Tsel = take(2, 384)
        top8 = take(NT, 8)
        iws = take(NT, IDX_H)
        xflat = xs.rearrange("p t d -> p (t d)")
        take = carver(xflat, NT * D)
        lora = take(NT, MLA_Q + MLA_KV)
        kdup = take(2, NT, P)
        take = carver(xflat, NT * D)
        qcat = take(NT, MLA_H, QK)
        rope4 = take(4, NT * MLA_H * ROPE // 2)
        kr4 = take(4, NT, ROPE // 2)
        take = carver(work, WORK)
        gact = take(2, 512)
        hid = take(2, 512)
        take = carver(work, WORK)
        onehot = take(2, 512)
        tables = take(NROWS)
        rrows = take(2, 512)
        KEPT = 2 * 512 * 2 + NSA_H * S + NT * NSA_H * NCMP
        take = carver(work[:, WORK - KEPT:WORK], KEPT)
        memkT = take(DEPTH, 2, S)
        vmem = take(DEPTH, NT, MEM_W)
        Tnsa = take(NSA_H, S)
        Tcmp = take(NT, NSA_H, NCMP)
        take = carver(work[:, 2048:WORK - KEPT], WORK - KEPT - 2048)
        memrows = take(NT, D)
        Gnsa = take(NSA_H, 384)
        final_bc = take(D)
        take = carver(work, 2048 + 2048)
        mkv = [take(NT, 2 * MEM_W) for _ in range(DEPTH)]
        take = carver(work[:, WORK - KEPT - 1200:WORK - KEPT], 1200)
        kmem = take(DEPTH, NT, MEM_W)
        take = carver(work, WORK - KEPT)
        z0 = take(NT, A_IN)
        vconv = take(6, S + 2)
        bconv = take(6, S)
        yconv = take(6, S)
        mq0 = take(2, S)
        take = carver(work, WORK - KEPT)
        kv = take(NT, 6 * NSA_G * HD)
        z1 = take(NT, B_IN)
        q8 = take(8, S)
        cmpT = take(2 * NSA_G, S)
        keysT = take(2 * NSA_G, S)
        w2 = take(2, 2, HD)
        kvc = take(2 * NSA_G, HD)
        kcd = take(NSA_G, 2 * HD)
        kcT = take(NSA_G, 2, 16)
        gate = take(NT, 3 * NSA_H)
        part = take(512)
        act_hid = part.rearrange("p (w n) -> p w n", w=2)
        cmax = take(NT * NSA_H)
        csum = take(NT * NSA_H)
        kd4 = q8.rearrange("p b s -> p (b s)").rearrange("p (t j g e) -> p t j g e", t=NT, j=4, g=NSA_G)
        gel4 = cmpT.rearrange("p b s -> p (b s)").rearrange("p (w j g e) -> p w j g e", w=2, j=2, g=NSA_G)
        vdiag = cmpT.rearrange("p b s -> p (b s)")[:, 0:NSA_H * HD].rearrange("p (a d) -> p a d", a=NSA_H)
        flat = xflat[:, 0:2 * 480].rearrange("p (w l g c) -> p w l g c", w=2, l=16, g=NSA_G)
        flatR = [[hT[:, part_, 2 * w:2 * w + 2, :].rearrange("p b s -> p (b s)")[:, 0:480] for w in range(2)]
                 for part_ in range(2)]
        LbF, PbF, PTbF = [b.rearrange("p a b -> p (a b)") for b in (Lb, Pb, PTb)]
        sbL = [LbF[:, 0:384], LbF[:, 384:768], PbF[:, 0:384], PbF[:, 384:768], PTbF[:, 0:384]]
        sbN = [PTbF[:, 384:768], xs[:, 0, 0:384], xs[:, 1, 0:384], Tsel[:, 0, :], Tsel[:, 1, :]]
        SB_BANK = (0, 1, 2, 3, 6)

        names = """cst_in onehot_in p_in_s final_in_s rows_out toep_in out_done hi_ready lo_ready piece_used
            sq_done ms_done rstd_ready xs_ready tr_done xhi xlo h_ready h_init tab_mm tab_ev toep_ready flipped
            wide_a wide_d tt_done tt_a tt_d dup_ready lora_ready cat_a cat_d rope_ready iws_ready
            s_done l_done e_done pt_done pte_done o_done o_evac
            tok0_done ix_s ix_r ix_a m_ready tm_ready sb_z sb_a sb_l sb_nl sb_s sb_w sb_e
            ff_sg ff_hid ff_hi ff_lo sig_done phi plo exp_set
            mem_in gn_in w2_in fn fn_ev hn_sq hn_r kn_ready v_ready qn_ready conv_y kd_ready flat_ready fhi flo
            gel_done gel_t rep_done kc_mm kcd_ready vd_ready kct_mm kct_ready gat_done cs_done cl_done ce_done ct_done cte_d cte_a
            a_chain d_chain g_chain uq_a uq_d ukv_a ukv_d""".split()
        E = {n: sem(n) for n in names}
        raw_in = [sem(f"raw_in{i}") for i in range(RR)]

        block = ctx.enter_context(nc.Block())



        class Unit:

            def __init__(self, srcs, dst, w, gain=None, shifted=False):
                self.srcs, self.dst, self.w, self.gain, self.shifted = srcs, dst, w, gain, shifted

            def moves(self, T):
                src = PS[T % 4][0:self.w, 0:len(self.srcs) * S].rearrange("p (b s) -> p b s", s=S)
                if not self.shifted:
                    return [(self.dst, src)]
                return [(self.dst[0:HD], src[0:HD]), (self.dst[HD:P, :, 0:S - 1], src[HD:P, :, 1:S])]

        def plain(src, c0, blocks, dst, gain=None):
            return [Unit([(lambda t, c=c0 + P * (b + j): src[:, t, c:c + P], P) for j in range(2)],
                         dst[:, b:b + 2, :], P, gain) for b in range(0, blocks, 2)]

        def mem_units():
            return [u for l in range(DEPTH)
                    for u in plain(kmem[:, l, :, :], 0, 2, memkT[:, l, :, :], COLS[("mem_k_gain_2", l)])]

        def conv_units():
            return plain(z0, 0, 6, bconv) + plain(z0, 2 * CONV, 6, vconv[:, :, 2:S + 2])

        def mem_query_units():
            return plain(z0, 3 * CONV, 2, mq0, COLS[("mem_q_gain_2", 0)])

        def kv_units():
            out_ = []
            for j in range(4):
                srcs = [(lambda t, j=j, g=g: kd4[:, t, j, g, :], P) for g in range(NSA_G)]
                if j < 2:
                    out_.append(Unit(srcs, cmpT[:, NSA_G * j:NSA_G * j + NSA_G, :], P, shifted=True))
                else:
                    out_.append(Unit(srcs, keysT[:, NSA_G * (j - 2):NSA_G * (j - 1), :], P,
                                     COLS[("k_gain_2", j - 1)]))
            return out_

        def query_units():
            return (plain(z1, 0, 6, q8[:, 0:6, :], COLS[("b_q_gain_2", 0)])
                    + plain(z1, NSA_H * HD + 3 * NSA_H, 2, q8[:, 6:8, :], COLS[("mem_q_gain_2", 1)]))

        def mem_jobs(l):
            q = mq0 if l == 0 else q8[:, 6:8, :]
            out_ = []
            for a in range(MEM_H):
                rr = slice((a % 2) * 64, (a % 2) * 64 + 64)
                out_.append(Job(q[rr, a // 2, :], memkT[rr, l, a // 2, :],
                                lambda kt, a=a: vmem[:, l, kt, HD * a:HD * a + HD], 1.0, None, CONV + HD * a,
                                causal=False))
            return out_

        def nsa_jobs(which):
            out_ = []
            for a in range(NSA_H):
                rr = slice((a % 2) * 64, (a % 2) * 64 + 64)
                c = (3 + 2 * which) * NSA_G * HD + a // HPG * HD
                out_.append(Job(q8[rr, a // 2, :], keysT[rr, NSA_G * which + a // HPG, :],
                                lambda kt, c=c: kv[:, kt, c:c + HD], 1.0, (Tnsa[:, a, 0:S], Tnsa[:, a, P:S]),
                                HD * a, gate=(a, 1 + which)))
            return out_

        def proj_units():
            def cols(c0, w):
                return [(lambda t, c=c0 + j: proj[:, t, c:c + min(P, c0 + w - c)], min(P, w - j)) for j in range(0, w, P)]
            units = []
            blk = 0
            for group in (cols(O_IQ, 512)[0:2], cols(O_IQ, 512)[2:4],
                          [(lambda t: kdup[:, 0, t, :], P), (lambda t: kdup[:, 1, t, :], P)],
                          cols(O_DQ, 320)[0:2], cols(O_DQ, 320)[2:3], cols(O_SQ, 320)[0:2], cols(O_SQ, 320)[2:3],
                          cols(O_SK, 320)[0:2], cols(O_SK, 320)[2:3]):
                w = group[0][1]
                units.append(Unit(group, allT[0:w, blk:blk + len(group), :], w))
                blk += len(group)
            return units

        B_IQ, B_IK, B_DK, B_DQ, B_SQ, B_SK = 0, 4, 5, 6, 9, 12

        def cat_units():
            units = []
            for src, dst in ((qcat, qT), (kcat, kT)):
                for hh in range(0, MLA_H, 2):
                    units.append(Unit([(lambda t, s=src, a=a: s[:, t, a, :], QK) for a in (hh, hh + 1)],
                                      dst[0:QK, hh:hh + 2, :], QK))
            return units

        def o_before(head0, i):
            return head0 + max(i - 1, 0)

        class Job:

            def __init__(self, q, k, v, scale, bias, dst, causal=True, selected=None, gate=None):
                self.gate = gate
                self.selected = selected
                self.q, self.k, self.v, self.scale, self.bias, self.dst = q, k, v, scale, bias, dst
                self.causal = causal

        def mla_jobs():
            return [Job(qT[0:QK, a, :], kT[0:QK, a, :], lambda kt, a=a: vmla[:, kt, a, :], QK ** -0.5,
                        (Tdsa[:, DSA_H, 0:S], Tdsa[:, DSA_H, P:S]), VDIM * a) for a in range(MLA_H)]

        def dsa_jobs():
            out_ = []
            for a in range(DSA_H):
                r = slice((a % 2) * 64, (a % 2) * 64 + 64)
                out_.append(Job(allT[r, B_DQ + a // 2, :], allT[r, B_DK, :],
                                lambda kt: proj[:, kt, O_DV:O_DV + HD], HD ** -0.5, None, MIX_DSA + HD * a, selected=a))
            return out_

        def groups(jobs):
            return [jobs[i:i + 4] for i in range(0, len(jobs), 4)]

        def spans(t, causal):
            if not causal:
                return t * S, S
            return (0, S) if t == 1 else (S, P)

        @block.sync
        def _(sp):
            sp.dma_start(cst[:, :], consts_in).then_inc(E["cst_in"], 16)
            sp.dma_start(col[:, :], cols_in).then_inc(E["cst_in"], 16)
            sp.dma_start(h[:, :, :], x_in.rearrange("(t p) d -> p t d", p=P)).then_inc(E["h_init"], 16)
            sp.dma_start(onehot[0:BUCKETS + 1, :, :], onehot_in).then_inc(E["onehot_in"], 16)
            sp.dma_start(tables[0:BUCKETS + 1, :], tables_in).then_inc(E["onehot_in"], 16)

            def load(p0, p1):
                for p in range(p0, p1):
                    name, layer, k0, nk, c0, w = PIECES[p]
                    if p >= RR:
                        sp.wait_ge(E["lo_ready"], p - RR + 1)
                    src = weights[name][layer, k0 * P:(k0 + nk) * P, c0:c0 + w].rearrange("(k p) n -> p k n", p=P)
                    dst = raw[:, p % RR, 0:nk * w].rearrange("p (k n) -> p k n", k=nk)
                    sp.dma_start(dst, src).then_inc(raw_in[p % RR], 16)

            load(0, RR)
            sp.wait_ge(E["tab_ev"], 2)
            sp.dma_start(R_dram.ap()[0:DSA_H + 1, :], rrows[0:DSA_H + 1, 0, :]).then_inc(E["rows_out"], 16)
            sp.dma_start(R_dram.ap()[DSA_H + 1:NROWS, :], rrows[0:NSA_H, 1, :]).then_inc(E["rows_out"], 16)
            sp.wait_ge(E["rows_out"], 32)
            for a in range(DSA_H + 1):
                sp.dma_start(Tdsa[:, a, :], bass.AP(R_dram, a * 512, [[1, P], [1, S]])).then_inc(E["toep_in"], 16)
            for l in range(DEPTH):
                load(RR if l == 0 else FIRST[("w_in", l)], FIRST[("ple_gate", l)])
                if l:
                    sp.wait_ge(E["plo"], l)
                sp.dma_start(pT[:, :, :], p_in[l].rearrange("(k p) s -> p k s", p=P)).then_inc(E["p_in_s"], 16)
                load(FIRST[("ple_gate", l)], FIRST[("w_in", l + 1)] if l + 1 < DEPTH else FIRST[("ple_proj", l)])
            sp.wait_ge(E["h_ready"], 10 * (DEPTH - 1) + 4)
            sp.dma_start(final_bc, final_in.partition_broadcast(P)).then_inc(E["final_in_s"], 16)
            sp.dma_start(memrows, mem_in.rearrange("(t p) d -> p t d", p=P)).then_inc(E["mem_in"], 16)
            for a in range(NSA_H):
                sp.dma_start(Gnsa[:, a, :], bass.AP(R_dram, (DSA_H + 1 + a) * 512, [[1, P], [1, 384]])
                             ).then_inc(E["gn_in"], 16)
            load(FIRST[("ple_proj", DEPTH - 1)], FIRST[("cmp", 0)])
            load(FIRST[("cmp", 0)], FIRST[("w_out", 1)])
            sp.dma_start(w2[:, :, :, :], w2_in.rearrange("w (j p) d -> p w j d", p=P)).then_inc(E["w2_in"], 16)
            load(FIRST[("w_out", 1)], len(PIECES))
            sp.wait_ge(E["h_ready"], 10 * DEPTH + 8 * DEPTH)
            sp.dma_start(out.rearrange("(t p) d -> p t d", p=P), h[:, :, :]).then_inc(E["out_done"], 16)
            sp.wait_ge(E["out_done"], 16)

        @block.gpsimd
        def _(pool):
            n = dict(chain=0, sq=0, hn=0)

            def link(ins):
                n["chain"] += 1
                ins.then_inc(E["g_chain"], 1)
                pool.wait_ge(E["g_chain"], n["chain"])

            def rsqrt_mean(widths):
                if len(widths) == 1:
                    for t in range(NT):
                        n["sq"] += 1
                        pool.wait_ge(E["sq_done"], n["sq"])
                        link(nc.gpsimd.tensor_scalar(ms[:, t:t + 1], ss[:, t:t + 1], 1.0 / widths[0], EPS,
                                                     ALU.mult, ALU.add))
                        nc.gpsimd.tensor_tensor(rstd[:, t:t + 1], ms[:, t:t + 1], expo[:, t:t + 1], ALU.pow
                                                ).then_inc(E["rstd_ready"], 1)
                    return
                n["sq"] += NT * len(widths)
                pool.wait_ge(E["sq_done"], n["sq"])
                for s, w in enumerate(widths):
                    i = nc.gpsimd.tensor_scalar(ms[:, NT * s:NT * s + NT], ss[:, NT * s:NT * s + NT], 1.0 / w, EPS,
                                                ALU.mult, ALU.add)
                    link(i)
                m = NT * len(widths)
                nc.gpsimd.tensor_tensor(rstd[:, 0:m], ms[:, 0:m], expo[:, 0:m], ALU.pow).then_inc(E["rstd_ready"], 1)

            def head_rsqrt(m):
                n["hn"] += 1
                pool.wait_ge(E["hn_sq"], n["hn"])
                link(nc.gpsimd.tensor_scalar(hms[:, 0:m], hss[:, 0:m], 1.0 / HD, EPS, ALU.mult, ALU.add))
                nc.gpsimd.tensor_tensor(hrs[:, 0:m], hms[:, 0:m], expo[:, 0:m], ALU.pow).then_inc(E["hn_r"], 1)

            link(nc.gpsimd.memset(expo[:, :], -0.5))
            for l in range(DEPTH):
                rsqrt_mean([D])
                rsqrt_mean([MLA_Q, MLA_KV])
                pool.wait_ge(E["toep_ready"], 3)
                pool.wait_ge(E["m_ready"], l + 1)
                for a in range(DSA_H):
                    J = l * (MLA_H + DSA_H) + MLA_H + a
                    if a >= 2:
                        pool.wait_ge(E["l_done"], NT * (J - 1))
                    nc.gpsimd.tensor_tensor(Tsel[:, a % 2, 0:S], Tdsa[:, a, 0:S], selm[:, 0:S], ALU.add)
                    nc.gpsimd.tensor_tensor(Tsel[:, a % 2, S:384], Tdsa[:, a, P:S], selm[:, S:384],
                                            ALU.add).then_inc(E["tm_ready"], 1)
                rsqrt_mean([D])
                rsqrt_mean([D])
            rsqrt_mean([D])
            rsqrt_mean([D])
            rsqrt_mean([D])
            head_rsqrt(DEPTH * NT * MEM_H)
            head_rsqrt(NT * MEM_H)
            rsqrt_mean([D])
            rsqrt_mean([D])
            head_rsqrt(2 * NT * NSA_G)
            head_rsqrt(NT * (NSA_H + MEM_H))
            head_rsqrt(NSA_G)
            rsqrt_mean([D])

        @block.scalar
        def _(act):
            n = dict(chain=0, split=0, tr=0, x=0, wide=0, T=0, J=0, B=0, X=0, F=0, G=0, O=0)

            def link(ins):
                n["chain"] += 1
                ins.then_inc(E["a_chain"], 1)
                act.wait_ge(E["a_chain"], n["chain"])

            def split_upto(limit):
                while n["split"] < min(limit, len(PIECES)):
                    p = n["split"]
                    act.wait_ge(raw_in[p % RR], 16 * (p // RR + 1))
                    if p >= RH:
                        act.wait_ge(E["piece_used"], p - RH + 1)
                    nc.scalar.activation(w_hi[:, p % RH, 0:piece_width(p)], raw[:, p % RR, 0:piece_width(p)],
                                         ACT.Copy).then_inc(E["hi_ready"], 1)
                    n["split"] += 1

            def squares(segments, ready=0, step=0):
                for s, seg in enumerate(segments):
                    for t in range(NT):
                        if step:
                            act.wait_ge(E["h_ready"], ready + step * (t + 1))
                        place = (Lb, Pb)[t].rearrange("p a b -> p (a b)")[:, 512 * s:512 * s + seg.shape[2]]
                        nc.scalar.activation(place, seg[:, t, :],
                                             ACT.Square, accum_out=ss[:, NT * s + t:NT * s + t + 1]
                                             ).then_inc(E["sq_done"], 1)

            def rounded_T(kn, dst, gain, at=0):
                for k in range(kn):
                    if k % 2 == 0:
                        n["tr"] += 1
                        act.wait_ge(E["tr_done"], n["tr"])
                    src = PS[k // 2 % 4][:, (k % 2) * S:(k % 2) * S + S]
                    if gain is None:
                        i = nc.scalar.activation(dst[:, 0, at + k, :], src, ACT.Copy)
                    else:
                        i = nc.scalar.activation(dst[:, 0, at + k, :], src, ACT.Copy, scale=col[:, gain[k]:gain[k] + 1])
                    i.then_inc(E["xhi"], 1)

            def evac_units(units):
                for u in units:
                    if n["T"] % 2 == 0:
                        act.wait_ge(E["tt_done"], n["T"] + 1)
                        for dst, src in u.moves(n["T"]):
                            i = nc.scalar.activation(dst, src, ACT.Copy,
                                                     scale=1.0 if u.gain is None else col[:, u.gain:u.gain + 1])
                        i.then_inc(E["tt_a"], 1)
                    n["T"] += 1

            def norm(kn, gain):
                squares([h[:, :, :]])
                rounded_T(kn, xT, gain)

            def wide_evac(stage, width, dst):
                p = FIRST[stage]
                for c0 in range(0, width, 512):
                    w = min(512, width - c0)
                    last = p + (2 if w > 256 else 1)
                    for q in range(p, last - 1):
                        split_upto(q + 1 + RH)
                    act.wait_ge(E["piece_used"], last)
                    nc.scalar.activation(dst[:, 0, c0:c0 + w], PS[4 + 2 * (n["wide"] % 2)][:, 0:w],
                                         ACT.Copy).then_inc(E["wide_a"], 1)
                    split_upto(last + RH)
                    p = last
                    n["wide"] += 1

            def attention(jobs):
                def exps(i):
                    job, J = jobs[i], n["J"] + i
                    b = J % 2
                    for t in (1, 0):
                        c, nk = spans(t, job.causal)
                        act.wait_ge(E["l_done"], NT * J + (2 - t if job.causal else NT))
                        G = n["G"] + i // 4
                        if i % 4 == 0 and t == 1 and G > 1:
                            act.wait_ge(E["o_evac"], G - 1)
                        if J >= 2:
                            act.wait_ge(E["pt_done"], J - 1)
                        src = Lb[:, b, c:c + nk] if job.causal else PS[b][:, c:c + nk]
                        nc.scalar.activation(Pb[:, b, c:c + nk], src, ACT.Exp, bias=nmax[:, b, t:t + 1],
                                             scale=-1.0 if job.causal else 1.0, accum_out=rows[:, 4 * (G % 2) + i % 4, t:t + 1]).then_inc(E["e_done"], 1)

                for i in range(len(jobs)):
                    exps(i)
                n["J"] += len(jobs)
                n["O"] += len(jobs)
                n["G"] += len(groups(jobs))

            def index_scores():
                for a in range(IDX_H):
                    X = n["X"]
                    act.wait_ge(E["ix_s"], X + 1)
                    if X >= 2:
                        act.wait_ge(E["ix_a"], X - 1)
                    nc.scalar.activation(Lb[:, X % 2, 0:384], PS[X % 2][:, 0:384], ACT.Relu,
                                         scale=HD ** -0.5).then_inc(E["ix_r"], 1)
                    n["X"] += 1

            def stick_breaking():
                B0 = n["B"]
                act.wait_ge(E["ix_a"], n["X"])
                for i in range(SB_H):
                    act.wait_ge(E["sb_z"], B0 + i + 1)
                    nc.scalar.activation(sbL[i], PS[SB_BANK[i]][:, 0:384], ACT.Abs, scale=HD ** -0.5
                                         ).then_inc(E["sb_a"], 1)
                act.wait_ge(E["sb_a"], B0 + SB_H)
                for i in range(SB_H):
                    last = nc.scalar.activation(sbL[i], sbL[i], ACT.Exp, scale=-1.0)
                link(last)
                for i in range(SB_H):
                    nc.scalar.activation(sbL[i], sbL[i], ACT.Ln, bias=1.0).then_inc(E["sb_l"], 1)
                for i in range(SB_H):
                    act.wait_ge(E["sb_w"], B0 + i + 1)
                    nc.scalar.activation(sbL[i], sbL[i], ACT.Exp).then_inc(E["sb_e"], 1)
                n["B"] += SB_H
                n["G"] += 2
                n["O"] += SB_H

            def mlp(stage, blocks, func, gated):
                p = FIRST[stage]
                per_up = 2 if gated else 1
                ups, downs = ffn_places(p, blocks, per_up)
                for c in range(blocks):
                    F = n["F"]
                    b = c % 2
                    if c == 0 and not gated:
                        split_upto(ups[0] + RH)
                    act.wait_ge(E["piece_used"], ups[c] + 1)
                    if F >= 2:
                        act.wait_ge(E["ff_hid"], F - 1)
                    nc.scalar.activation(gact[:, b, :], PS[2 * b][:, :], func).then_inc(E["ff_sg"], 1)
                    split_upto(ups[c] + per_up + RH - 1)
                    act.wait_ge(E["ff_hid"], F + 1)
                    if c >= 2:
                        act.wait_ge(E["piece_used"], downs[c - 2] + 1)
                    nc.scalar.activation(hT[:, 0, 2 * b:2 * b + 2, :], hid[:, b, :].rearrange("p (k s) -> p k s", k=2),
                                         ACT.Copy).then_inc(E["ff_hi"], 1)
                    split_upto(ups[c] + per_up + RH)
                    if c:
                        split_upto(downs[c - 1] + 1 + RH)
                    n["F"] += 1
                split_upto(downs[-1] + 1 + RH)

            act.wait_ge(E["cst_in"], 32)
            act.wait_ge(E["h_init"], 16)
            for l in range(DEPTH):
                squares([h[:, :, :]], 10 * l - 2, 1 if l else 0)
                if l == 0:
                    split_upto(RH)
                    act.wait_ge(E["tab_mm"], 1)
                    nc.scalar.activation(rrows[0:NSA_H, 1, :], PS[5][0:NSA_H, :], ACT.Copy).then_inc(E["tab_ev"], 1)
                rounded_T(KD, xT, gains(("attn_norm", l), KD))
                if l == 0:
                    act.wait_ge(E["rows_out"], 32)
                wide_evac(("w_in", l), D_IN, proj)
                act.wait_ge(E["wide_d"], n["wide"])
                squares([proj[:, :, O_CQ:O_CQ + MLA_Q], proj[:, :, O_CKV:O_CKV + MLA_KV]])
                evac_units(proj_units())
                rounded_T(5, hT, gains(("mla_q_norm", l), 3) + gains(("mla_kv_norm", l), 2))
                act.wait_ge(E["piece_used"], FIRST[("uq", l)] + 1)
                for half in range(2):
                    i = nc.scalar.activation(qcat[:, 0, 3 * half:3 * half + 3, :],
                                             PS[4 + half][:, 0:3 * QK].rearrange("p (a b) -> p a b", a=3), ACT.Copy)
                i.then_inc(E["uq_a"], 1)
                act.wait_ge(E["piece_used"], FIRST[("ukv", l)] + 1)
                for half in range(2):
                    heads = PS[half][:, 0:384].rearrange("p (a b) -> p a b", a=3)
                    nc.scalar.activation(kcat[:, 0, 3 * half:3 * half + 3, 0:NOPE], heads[:, :, 0:NOPE], ACT.Copy)
                    i = nc.scalar.activation(vmla[:, 0, 3 * half:3 * half + 3, :], heads[:, :, NOPE:NOPE + VDIM], ACT.Copy)
                i.then_inc(E["ukv_a"], 1)
                split_upto(FIRST[("ukv", l)] + 1 + RH)
                evac_units(cat_units())
                index_scores()
                stick_breaking()
                attention(mla_jobs() + dsa_jobs())
                rounded_T(KD, xT, None)
                for p in range(FIRST[("w_o", l)], FIRST[("w_o", l)] + 4):
                    split_upto(p + 1 + RH)
                squares([h[:, :, :]], 10 * l, 2)
                rounded_T(KD, xT, gains(("ffn_norm", l), KD))
                mlp(("ffn1", l), FF1 // 256, ACT.Silu, True)
                act.wait_ge(E["p_in_s"], 16 * (l + 1))
                nc.scalar.activation(hT[:, 0, 0:2, :], pT[:, :, :], ACT.Copy).then_inc(E["phi"], 1)
                squares([h[:, :, :]], 10 * l + 4, 2)
                rounded_T(KD, xT, gains(("ple_norm", l), KD))
                for p in range(FIRST[("ple_gate", l)], FIRST[("ple_gate", l)] + 4):
                    split_upto(p + 1 + RH)
                act.wait_ge(E["piece_used"], FIRST[("ple_proj", l)])
                for t in range(NT):
                    for c in range(2):
                        nc.scalar.activation(xs[:, t, 512 * c:512 * c + 512], PS[4 + 2 * t + c][:, :],
                                             ACT.Sigmoid).then_inc(E["sig_done"], 1)
                split_upto(FIRST[("ple_proj", l)] + 1 + RH)
            squares([h[:, :, :]], 10 * DEPTH - 2, 1)

            act.wait_ge(E["mem_in"], 16)
            act.wait_ge(E["rstd_ready"], 7 * DEPTH + 2)
            act.wait_ge(E["exp_set"], 2)
            squares([memrows])
            for j in range(9):
                act.wait_ge(E["fn"], j + 1)
                a0, seg = 4 * (j // 3), j % 3
                b = PS[j % 4][:, :].rearrange("p (a m) -> p a m", a=4)
                if seg < 2:
                    nc.scalar.activation(Tnsa[:, a0:a0 + 4, P * seg:P * seg + P], b, ACT.Copy)
                for t, base in ((1, CMP_LEN - 1), (0, CMP_LEN - 1 + P)):
                    cs = [c for c in range(NCMP) if (base + CMP_STRIDE * c) // P == seg]
                    if cs:
                        m0 = base + CMP_STRIDE * cs[0] - P * seg
                        i = nc.scalar.activation(Tcmp[:, t, a0:a0 + 4, cs[0]:cs[-1] + 1],
                                                 b[:, :, m0:m0 + CMP_STRIDE * (len(cs) - 1) + 1:CMP_STRIDE], ACT.Copy)
                i.then_inc(E["fn_ev"], 1)
            rounded_T(KD, xT, gains(("mem_norm_2", None), KD))
            for l in range(DEPTH):
                wide_evac(("mem_kv", l), 2 * MEM_W, mkv[l])
            for l in range(DEPTH):
                squares([h[:, :, :]], 10 * DEPTH + 4, 2 * l)
                if l == 0:
                    rounded_T(KD, xT, gains(("mix_norm_2", 0), KD))
                    act.wait_ge(E["kn_ready"], 1)
                    wide_evac(("a_in", 0), A_IN, z0)
                    evac_units(mem_units() + conv_units() + mem_query_units())
                    for b in range(6):
                        act.wait_ge(E["conv_y"], b + 1)
                        nc.scalar.activation(xT[:, 0, b, :], yconv[:, b, :], ACT.Copy).then_inc(E["xhi"], 1)
                    attention(mem_jobs(0))
                else:
                    rounded_T(KD, xT, gains(("kv_norm_2", None), KD))
                    wide_evac(("kv", 1), 6 * NSA_G * HD, kv)
                    rounded_T(KD, xT, gains(("mix_norm_2", 1), KD))
                    wide_evac(("b_in", 1), B_IN, z1)
                    act.wait_ge(E["wide_a"], n["wide"])
                    act.wait_ge(E["wide_d"], n["wide"])
                    nc.scalar.activation(gate[:, :, :], z1[:, :, NSA_H * HD:NSA_H * HD + 3 * NSA_H], ACT.Sigmoid
                                         ).then_inc(E["gat_done"], 1)
                    evac_units(kv_units())
                    act.wait_ge(E["flat_ready"], 1)
                    for w in range(2):
                        nc.scalar.activation(flatR[0][w], flat[:, w].rearrange("p l g c -> p (l g c)"), ACT.Copy
                                             ).then_inc(E["fhi"], 1)
                    for w in range(2):
                        act.wait_ge(E["piece_used"], FIRST[("cmp", w)] + 2)
                        nc.scalar.activation(act_hid[0:NSA_G * NCMP, w, :], PS[w][0:NSA_G * NCMP, 0:CMP_HID],
                                             ACT.Gelu_apprx_tanh).then_inc(E["gel_done"], 1)
                        split_upto(FIRST[("cmp", w)] + 2 + RH)
                    evac_units(query_units())
                    act.wait_ge(E["cl_done"], 1)
                    nc.scalar.activation(PbF[:, 0:768].rearrange("p (a c) -> p a c", c=32)[:, :, 0:NCMP],
                                         LbF[:, 0:768].rearrange("p (a c) -> p a c", c=32)[:, :, 0:NCMP], ACT.Exp
                                         ).then_inc(E["ce_done"], 1)
                    act.wait_ge(E["ct_done"], 2)
                    nc.scalar.activation(PTbF[:, 384:768], PS[2][:, 0:384], ACT.Copy).then_inc(E["cte_a"], 1)
                    n["G"] += 3
                    n["O"] += NSA_H
                    attention(nsa_jobs(0) + nsa_jobs(1))
                    attention(mem_jobs(1))
                rounded_T(2 if l == 0 else KD, xT, None, at=6 if l == 0 else 0)
                for p in range(FIRST[("w_out", l)], FIRST[("w_out", l)] + 4):
                    split_upto(p + 1 + RH)
                squares([h[:, :, :]], 10 * DEPTH + 8 * l, 2)
                rounded_T(KD, xT, gains(("mlp_norm_2", l), KD))
                mlp(("ffn2", l), FF2 // 256, ACT.Relu, False)

        @block.vector
        def _(dve):
            n = dict(chain=0, split=0, tr=0, x=0, wide=0, T=0, J=0, B=0, X=0, F=0, G=0, O=0, norm=0, tok0=0)

            def link(ins):
                n["chain"] += 1
                ins.then_inc(E["d_chain"], 1)
                dve.wait_ge(E["d_chain"], n["chain"])

            def split_upto(limit):
                while n["split"] < min(limit, len(PIECES)):
                    p = n["split"]
                    dve.wait_ge(E["hi_ready"], p + 1)
                    if p >= RH:
                        dve.wait_ge(E["piece_used"], p - RH + 1)
                    w = piece_width(p)
                    nc.vector.tensor_tensor(w_lo[:, p % RH, 0:w], raw[:, p % RR, 0:w],
                                            w_hi[:, p % RH, 0:w].bitcast(F32), ALU.subtract).then_inc(E["lo_ready"], 1)
                    n["split"] += 1

            def scaled(dsts, srcs):
                if len(dsts) == 1:
                    for t in range(NT):
                        n["norm"] += 1
                        dve.wait_ge(E["rstd_ready"], n["norm"])
                        nc.vector.tensor_scalar(dsts[0][:, t, :], srcs[0][:, t, :], rstd[:, t:t + 1], None, ALU.mult
                                                ).then_inc(E["xs_ready"], 1)
                    return
                n["norm"] += 1
                dve.wait_ge(E["rstd_ready"], n["norm"])
                for s, (dst, src) in enumerate(zip(dsts, srcs)):
                    for t in range(NT):
                        i = nc.vector.tensor_scalar(dst[:, t, :], src[:, t, :], rstd[:, NT * s + t:NT * s + t + 1],
                                                    None, ALU.mult)
                i.then_inc(E["xs_ready"], NT)

            def rest_T(kn, dst, gain, at=0):
                for k in range(kn):
                    if k % 2 == 0:
                        n["x"] += min(2, kn - k)
                        dve.wait_ge(E["xhi"], n["x"])
                    src = PS[k // 2 % 4][:, (k % 2) * S:(k % 2) * S + S]
                    hi = dst[:, 0, at + k, :].bitcast(F32)
                    if gain is None:
                        i = nc.vector.tensor_tensor(dst[:, 1, at + k, :], src, hi, ALU.subtract)
                    else:
                        i = nc.vector.scalar_tensor_tensor(dst[:, 1, at + k, :], src, col[:, gain[k]:gain[k] + 1], hi,
                                                           op0=ALU.mult, op1=ALU.subtract)
                    i.then_inc(E["xlo"], 1)

            def evac_units(units):
                for u in units:
                    if n["T"] % 2 == 1:
                        dve.wait_ge(E["tt_done"], n["T"] + 1)
                        for dst, src in u.moves(n["T"]):
                            if u.gain is None:
                                i = nc.vector.tensor_copy(dst, src)
                            else:
                                i = nc.vector.tensor_scalar(dst, src, col[:, u.gain:u.gain + 1], None, ALU.mult)
                        i.then_inc(E["tt_d"], 1)
                    n["T"] += 1

            def wide_evac(stage, width, dst):
                p = FIRST[stage]
                for c0 in range(0, width, 512):
                    w = min(512, width - c0)
                    last = p + (2 if w > 256 else 1)
                    for q in range(p, last - 1):
                        split_upto(q + 1 + RH)
                    dve.wait_ge(E["piece_used"], last)
                    nc.vector.tensor_copy(dst[:, 1, c0:c0 + w],
                                          PS[5 + 2 * (n["wide"] % 2)][:, 0:w]).then_inc(E["wide_d"], 1)
                    split_upto(last + RH)
                    p = last
                    n["wide"] += 1

            def outputs(dsts, J0, factor, gated=None):
                G = n["G"]
                m = len(dsts)
                dve.wait_ge(E["o_done"], J0 + m)
                src = PS[4 + G % 2][:, 0:m * NT * HD].rearrange("p (a t d) -> p a t d", a=m, t=NT)
                dst = xs[:, :, dsts[0]:dsts[0] + m * HD].rearrange("p t (a d) -> p a t d", a=m)
                f = rinv[:, 0:m, :]
                if isinstance(factor, str):
                    r0 = 4 * (G % 2)
                    link(nc.vector.reciprocal(f, rows[:, r0:r0 + m, :]))
                    factor = f
                if gated is not None:
                    if G:
                        dve.wait_ge(E["o_evac"], G)
                    a, branch = gated
                    g = gate[:, :, :].rearrange("p t (a e) -> p a t e", e=3)[:, a:a + m, :, branch]
                    link(nc.vector.tensor_tensor(f, factor, g, ALU.mult))
                fb = f.unsqueeze(3).broadcast_to([P, m, NT, HD])
                if factor is None:
                    i = nc.vector.tensor_copy(dst, src)
                elif gated is None or gated[1] == 0:
                    i = nc.vector.tensor_tensor(dst, src, fb, ALU.mult)
                else:
                    pv = part[:, 0:m * NT * HD].rearrange("p (a t d) -> p a t d", a=m, t=NT)
                    link(nc.vector.tensor_tensor(pv, src, fb, ALU.mult))
                    i = nc.vector.tensor_tensor(dst, dst, pv, ALU.add)
                i.then_inc(E["o_evac"], 1)
                n["G"] += 1

            def attention(jobs):
                o0 = n["O"]

                def logits(i):
                    job, J = jobs[i], n["J"] + i
                    b = J % 2
                    dve.wait_ge(E["s_done"], J + 1)
                    if J >= 2:
                        dve.wait_ge(E["e_done"], NT * (J - 1))
                    if job.selected is not None:
                        a = job.selected
                        dve.wait_ge(E["tm_ready"], J // (MLA_H + DSA_H) * DSA_H + a + 1)
                        bias = (Tsel[:, a % 2, 0:S], Tsel[:, a % 2, S:384])
                    else:
                        bias = job.bias
                    for t in (1, 0):
                        c, nk = spans(t, job.causal)
                        if not job.causal:
                            nc.vector.tensor_reduce(nmax[:, b, t:t + 1], PS[b][:, c:c + nk], AX_X, ALU.max, negate=True
                                                    ).then_inc(E["l_done"], 1)
                            continue
                        nc.vector.tensor_tensor_reduce(out=Lb[:, b, c:c + nk], in0=PS[b][:, c:c + nk],
                                                       in1=bias[1 - t], scale=-job.scale, scalar=3e38, op0=ALU.add,
                                                       op1=ALU.min, accum_out=nmax[:, b, t:t + 1]
                                                       ).then_inc(E["l_done"], 1)

                def move_pT(i):
                    J = n["J"] + i
                    b = J % 2
                    dve.wait_ge(E["pt_done"], J + 1)
                    if o_before(o0, i):
                        dve.wait_ge(E["o_done"], o_before(o0, i))
                    w = 384 if jobs[i].causal else 512
                    nc.vector.tensor_copy(PTb[:, b, 0:w], PS[2 + b][:, 0:w]).then_inc(E["pte_done"], 1)

                logits(0)
                for i in range(len(jobs)):
                    if i + 1 < len(jobs):
                        logits(i + 1)
                    move_pT(i)
                    if i % 4 == 0 and i:
                        outputs([jobs[j].dst for j in range(i - 4, i)], o0 + i - 4, "rows", jobs[i - 4].gate)
                g = (len(jobs) - 1) // 4 * 4
                outputs([jobs[j].dst for j in range(g, len(jobs))], o0 + g, "rows", jobs[g].gate)
                n["J"] += len(jobs)
                n["O"] += len(jobs)

            def index_scores():
                for a in range(IDX_H):
                    X = n["X"]
                    dve.wait_ge(E["ix_r"], X + 1)
                    if a:
                        dve.wait_ge(E["ix_a"], X)
                    for t in (1, 0):
                        c, nk = spans(t, True)
                        src, w = Lb[:, X % 2, c:c + nk], iws[:, t, a:a + 1]
                        if a == 0:
                            i = nc.vector.tensor_scalar(isc[:, c:c + nk], src, w, None, ALU.mult)
                        else:
                            i = nc.vector.scalar_tensor_tensor(isc[:, c:c + nk], src, w, isc[:, c:c + nk],
                                                               op0=ALU.mult, op1=ALU.add)
                    i.then_inc(E["ix_a"], 1)
                    n["X"] += 1
                dve.wait_ge(E["ix_a"], n["X"])
                dve.wait_ge(E["toep_ready"], 3)
                nc.vector.tensor_tensor(isc[:, 0:S], isc[:, 0:S], Tdsa[:, DSA_H, 0:S], ALU.add)
                link(nc.vector.tensor_tensor(isc[:, S:384], isc[:, S:384], Tdsa[:, DSA_H, P:S], ALU.add))

            def select(l):
                for r in range(TOPK // 8):
                    for t in (1, 0):
                        c, nk = spans(t, True)
                        i = nc.vector.max(top8[:, t, :], isc[:, c:c + nk])
                    link(i)
                    for t in (1, 0):
                        c, nk = spans(t, True)
                        i = nc.vector.match_replace(isc[:, c:c + nk], top8[:, t, :], isc[:, c:c + nk], TAKEN)
                    link(i)
                nc.vector.tensor_scalar(selm[:, :], isc[:, :], TAKEN / 2, NEG, ALU.is_gt, ALU.mult
                                        ).then_inc(E["m_ready"], 1)

            def stick_breaking():
                B0, o0 = n["B"], n["O"]

                for i in range(SB_H):
                    dve.wait_ge(E["sb_a"], B0 + i + 1)
                    last = nc.vector.tensor_scalar(sbN[i], PS[SB_BANK[i]][:, 0:384], 0.0, HD ** -0.5, ALU.max, ALU.mult)
                link(last)
                for i in range(SB_H):
                    dve.wait_ge(E["sb_l"], B0 + i + 1)
                    link(nc.vector.tensor_tensor(sbN[i], sbN[i], sbL[i], ALU.add))
                    nc.vector.tensor_tensor(sbN[i], sbN[i], negm, ALU.mult).then_inc(E["sb_nl"], 1)
                for i in range(SB_H):
                    dve.wait_ge(E["sb_s"], B0 + i + 1)
                    nc.vector.scalar_tensor_tensor(sbL[i], PS[SB_BANK[i]][:, 0:384], HD ** -0.5, smask,
                                                   op0=ALU.mult, op1=ALU.add).then_inc(E["sb_w"], 1)
                outputs([MIX_SB + HD * a for a in range(4)], o0, None)
                outputs([MIX_SB + HD * 4], o0 + 4, None)
                n["B"] += SB_H
                n["O"] += SB_H

            def add_to_h(result):
                n["tok0"] += 1
                for t in range(NT):
                    if t == 0:
                        dve.wait_ge(E["tok0_done"], n["tok0"])
                    else:
                        dve.wait_ge(E["piece_used"], result)
                    for c in range(2):
                        nc.vector.tensor_tensor(h[:, t, 512 * c:512 * c + 512], h[:, t, 512 * c:512 * c + 512],
                                                PS[4 + 2 * t + c][:, :], ALU.add).then_inc(E["h_ready"], 1)

            def mlp(stage, blocks, gated):
                p = FIRST[stage]
                per_up = 2 if gated else 1
                ups, downs = ffn_places(p, blocks, per_up)
                for c in range(blocks):
                    F = n["F"]
                    b = c % 2
                    if c == 0 and not gated:
                        split_upto(ups[0] + RH)
                    dve.wait_ge(E["ff_sg"], F + 1)
                    split_upto(ups[c] + per_up + RH - 1)
                    dve.wait_ge(E["piece_used"], ups[c] + per_up)
                    if F >= 2:
                        dve.wait_ge(E["ff_lo"], F - 1)
                    nc.vector.tensor_tensor(hid[:, b, :], gact[:, b, :], PS[2 * b + per_up - 1][:, :], ALU.mult
                                            ).then_inc(E["ff_hid"], 1)
                    dve.wait_ge(E["ff_hi"], F + 1)
                    nc.vector.tensor_tensor(hT[:, 1, 2 * b:2 * b + 2, :],
                                            hid[:, b, :].rearrange("p (k s) -> p k s", k=2),
                                            hT[:, 0, 2 * b:2 * b + 2, :].bitcast(F32), ALU.subtract
                                            ).then_inc(E["ff_lo"], 1)
                    split_upto(ups[c] + per_up + RH)
                    if c:
                        split_upto(downs[c - 1] + 1 + RH)
                    n["F"] += 1
                split_upto(downs[-1] + 1 + RH)

            dve.wait_ge(E["cst_in"], 32)
            dve.wait_ge(E["h_init"], 16)
            for l in range(DEPTH):
                scaled([xs], [h])
                if l == 0:
                    split_upto(RH)
                    dve.wait_ge(E["tab_mm"], 1)
                    nc.vector.tensor_scalar(rrows[0:DSA_H + 1, 0, :], PS[4][0:DSA_H + 1, :], HD ** 0.5, None, ALU.mult
                                            ).then_inc(E["tab_ev"], 1)
                rest_T(KD, xT, gains(("attn_norm", l), KD))
                if l == 0:
                    dve.wait_ge(E["rows_out"], 32)
                wide_evac(("w_in", l), D_IN, proj)
                dve.wait_ge(E["wide_a"], n["wide"])
                if l == 0:
                    for j in range(3):
                        dve.wait_ge(E["flipped"], j + 1)
                        nc.vector.tensor_copy(Tdsa[:, 2 * j:2 * j + 2, :],
                                              PS[j][:, :].rearrange("p (a s) -> p a s", a=2)
                                              ).then_inc(E["toep_ready"], 1)
                for which, c0 in enumerate((O_IK, O_DK)):
                    i = nc.vector.tensor_copy(kdup[:, which, :, :].rearrange("p t (u d) -> p t u d", u=2),
                                              proj[:, :, c0:c0 + HD].unsqueeze(2).broadcast_to([P, NT, 2, HD]))
                i.then_inc(E["dup_ready"], 1)
                link(nc.vector.tensor_scalar(iws[:, :, :], proj[:, :, O_IW:O_IW + IDX_H], IDX_H ** -0.5, None, ALU.mult))
                scaled([lora[:, :, 0:MLA_Q], lora[:, :, MLA_Q:MLA_Q + MLA_KV]],
                       [proj[:, :, O_CQ:O_CQ + MLA_Q], proj[:, :, O_CKV:O_CKV + MLA_KV]])
                evac_units(proj_units())
                rest_T(5, hT, gains(("mla_q_norm", l), 3) + gains(("mla_kv_norm", l), 2))
                dve.wait_ge(E["piece_used"], FIRST[("uq", l)] + 1)
                for half in range(2):
                    i = nc.vector.tensor_copy(qcat[:, 1, 3 * half:3 * half + 3, :],
                                              PS[6 + half][:, 0:3 * QK].rearrange("p (a b) -> p a b", a=3))
                link(i)
                dve.wait_ge(E["uq_a"], l + 1)
                hf = ROPE // 2
                x1, x2 = qcat[:, :, :, NOPE:NOPE + hf], qcat[:, :, :, NOPE + hf:QK]
                r4 = [rope4[:, a, :].rearrange("p (t a f) -> p t a f", t=NT, a=MLA_H) for a in range(4)]
                cb = cos.unsqueeze(2).broadcast_to([P, NT, MLA_H, hf])
                sn = sin.unsqueeze(2).broadcast_to([P, NT, MLA_H, hf])
                for a, (u, v) in enumerate(((x1, cb), (x2, sn), (x1, sn), (x2, cb))):
                    nc.vector.tensor_tensor(r4[a], u, v, ALU.mult)
                k1, k2 = proj[:, :, O_KR:O_KR + hf], proj[:, :, O_KR + hf:O_KR + ROPE]
                for a, (u, v) in enumerate(((k1, cos), (k2, sin), (k1, sin), (k2, cos))):
                    i = nc.vector.tensor_tensor(kr4[:, a, :, :], u, v, ALU.mult)
                link(i)
                nc.vector.tensor_tensor(x1, r4[0], r4[1], ALU.subtract)
                nc.vector.tensor_tensor(x2, r4[2], r4[3], ALU.add)
                kb = [kr4[:, a, :, :].unsqueeze(2).broadcast_to([P, NT, MLA_H, hf]) for a in range(4)]
                nc.vector.tensor_tensor(kcat[:, :, :, NOPE:NOPE + hf], kb[0], kb[1], ALU.subtract)
                nc.vector.tensor_tensor(kcat[:, :, :, NOPE + hf:QK], kb[2], kb[3], ALU.add)
                dve.wait_ge(E["piece_used"], FIRST[("ukv", l)] + 1)
                for half in range(2):
                    heads = PS[2 + half][:, 0:384].rearrange("p (a b) -> p a b", a=3)
                    nc.vector.tensor_copy(kcat[:, 1, 3 * half:3 * half + 3, 0:NOPE], heads[:, :, 0:NOPE])
                    i = nc.vector.tensor_copy(vmla[:, 1, 3 * half:3 * half + 3, :], heads[:, :, NOPE:NOPE + VDIM])
                i.then_inc(E["ukv_d"], 1)
                split_upto(FIRST[("ukv", l)] + 1 + RH)
                evac_units(cat_units())
                index_scores()
                stick_breaking()
                select(l)
                attention(mla_jobs() + dsa_jobs())
                rest_T(KD, xT, None)
                for p in range(FIRST[("w_o", l)], FIRST[("w_o", l)] + 4):
                    split_upto(p + 1 + RH)
                add_to_h(FIRST[("w_o", l)] + 4)
                scaled([xs], [h])
                rest_T(KD, xT, gains(("ffn_norm", l), KD))
                mlp(("ffn1", l), FF1 // 256, True)
                dve.wait_ge(E["phi"], l + 1)
                nc.vector.tensor_tensor(hT[:, 1, 0:2, :], pT[:, :, :], hT[:, 0, 0:2, :].bitcast(F32), ALU.subtract
                                        ).then_inc(E["plo"], 1)
                add_to_h(FIRST[("ple_gate", l)])
                scaled([xs], [h])
                rest_T(KD, xT, gains(("ple_norm", l), KD))
                for p in range(FIRST[("ple_gate", l)], FIRST[("ple_gate", l)] + 4):
                    split_upto(p + 1 + RH)
                split_upto(FIRST[("ple_proj", l)] + 1 + RH)
                dve.wait_ge(E["sig_done"], 4 * (l + 1))
                dve.wait_ge(E["piece_used"], FIRST[("ple_proj", l)] + 1)
                for t in range(NT):
                    for c in range(2):
                        x = xs[:, t, 512 * c:512 * c + 512]
                        i = nc.vector.tensor_tensor(x, x, PS[2 * t + c][:, :], ALU.mult)
                link(i)
                for t in range(NT):
                    i = nc.vector.tensor_tensor(h[:, t, :], h[:, t, :], xs[:, t, :], ALU.add)
                    i.then_inc(E["h_ready"], 1)
            dve.wait_ge(E["final_in_s"], 16)
            for t in range(NT):
                n["norm"] += 1
                dve.wait_ge(E["rstd_ready"], n["norm"])
                nc.vector.scalar_tensor_tensor(h[:, t, :], h[:, t, :], rstd[:, t:t + 1], final_bc[:, :], op0=ALU.mult,
                                               op1=ALU.mult).then_inc(E["exp_set"], 1)

            dve.wait_ge(E["exp_set"], 2)
            scaled([xs], [memrows])
            rest_T(KD, xT, gains(("mem_norm_2", None), KD))
            for l in range(DEPTH):
                wide_evac(("mem_kv", l), 2 * MEM_W, mkv[l])
            dve.wait_ge(E["wide_a"], n["wide"])
            dve.wait_ge(E["wide_d"], n["wide"])
            for l in range(DEPTH):
                scaled([xs], [h])
                if l == 0:
                    rest_T(KD, xT, gains(("mix_norm_2", 0), KD))
                    for m in range(DEPTH):
                        i = nc.vector.tensor_tensor((LbF, PbF)[m][:, 0:512].rearrange("p (t d) -> p t d", t=NT),
                                                    mkv[m][:, :, 0:MEM_W], mkv[m][:, :, 0:MEM_W], ALU.mult)
                    link(i)
                    for m in range(DEPTH):
                        i = nc.vector.tensor_reduce(hss[:, 8 * m:8 * m + 8],
                                                    (LbF, PbF)[m][:, 0:512].rearrange("p (a d) -> p a d", d=HD), AX_X, ALU.add)
                        nc.vector.tensor_copy(vmem[:, m, :, :], mkv[m][:, :, MEM_W:2 * MEM_W])
                    i.then_inc(E["hn_sq"], 1)
                    dve.wait_ge(E["hn_r"], 1)
                    for m in range(DEPTH):
                        i = nc.vector.tensor_tensor(kmem[:, m, :, :].rearrange("p t (a d) -> p t a d", d=HD),
                                                    mkv[m][:, :, 0:MEM_W].rearrange("p t (a d) -> p t a d", d=HD),
                                                    hrs[:, 8 * m:8 * m + 8].rearrange("p (t a) -> p t a", t=NT).unsqueeze(3)
                                                    .broadcast_to([P, NT, MEM_H, HD]), ALU.mult)
                    i.then_inc(E["kn_ready"], 1)
                    wide_evac(("a_in", 0), A_IN, z0)
                    dve.wait_ge(E["wide_a"], n["wide"])
                    dve.wait_ge(E["wide_d"], n["wide"])
                    nc.vector.memset(vconv[:, :, 0:2], 0.0)
                    u = z0[:, :, 2 * CONV:3 * CONV]
                    nc.vector.tensor_tensor(u, z0[:, :, CONV:2 * CONV], u, ALU.mult).then_inc(E["v_ready"], 1)
                    mq = z0[:, :, 3 * CONV:A_IN]
                    link(nc.vector.tensor_tensor(LbF[:, 0:512].rearrange("p (t d) -> p t d", t=NT), mq, mq, ALU.mult))
                    nc.vector.tensor_reduce(hss[:, 0:8], LbF[:, 0:512].rearrange("p (a d) -> p a d", d=HD), AX_X,
                                            ALU.add).then_inc(E["hn_sq"], 1)
                    dve.wait_ge(E["hn_r"], 2)
                    for t in range(NT):
                        qv = mq[:, t, :].rearrange("p (a d) -> p a d", d=HD)
                        i = nc.vector.scalar_tensor_tensor(qv, qv, HD ** -0.5, hrs[:, 4 * t:4 * t + 4].unsqueeze(2)
                                                           .broadcast_to([P, MEM_H, HD]), op0=ALU.mult, op1=ALU.mult)
                    i.then_inc(E["qn_ready"], 1)
                    evac_units(mem_units() + conv_units() + mem_query_units())
                    dve.wait_ge(E["tt_a"], (n["T"] + 1) // 2)
                    dve.wait_ge(E["tt_d"], n["T"] // 2)
                    for k in range(3):
                        for b in range(6):
                            w = COLS[("a_conv_w_2", k)] + b
                            src, y = vconv[:, b, k:k + S], yconv[:, b, :]
                            if k == 0:
                                i = nc.vector.tensor_scalar(y, src, col[:, w:w + 1], None, ALU.mult)
                            else:
                                i = nc.vector.scalar_tensor_tensor(y, src, col[:, w:w + 1], y, op0=ALU.mult, op1=ALU.add)
                        link(i)
                    for b in range(6):
                        nc.vector.tensor_tensor(yconv[:, b, :], yconv[:, b, :], bconv[:, b, :], ALU.mult
                                                ).then_inc(E["conv_y"], 1)
                    for b in range(6):
                        n["x"] += 1
                        dve.wait_ge(E["xhi"], n["x"])
                        nc.vector.tensor_tensor(xT[:, 1, b, :], yconv[:, b, :], xT[:, 0, b, :].bitcast(F32),
                                                ALU.subtract).then_inc(E["xlo"], 1)
                    attention(mem_jobs(0))
                else:
                    rest_T(KD, xT, gains(("kv_norm_2", None), KD))
                    wide_evac(("kv", 1), 6 * NSA_G * HD, kv)
                    rest_T(KD, xT, gains(("mix_norm_2", 1), KD))
                    wide_evac(("b_in", 1), B_IN, z1)
                    dve.wait_ge(E["wide_a"], n["wide"])
                    dve.wait_ge(E["wide_d"], n["wide"])
                    kv5 = kv.rearrange("p t (j g d) -> p t j g d", j=6, g=NSA_G)
                    for jj, j in enumerate((2, 4)):
                        kk = kv[:, :, P * j:P * j + P]
                        i = nc.vector.tensor_tensor(LbF[:, S * jj:S * jj + S].rearrange("p (t d) -> p t d", t=NT), kk, kk,
                                                    ALU.mult)
                    link(i)
                    nc.vector.tensor_reduce(hss[:, 0:8], LbF[:, 0:512].rearrange("p (a d) -> p a d", d=HD), AX_X,
                                            ALU.add).then_inc(E["hn_sq"], 1)
                    for j in range(2):
                        for t in range(NT):
                            nc.vector.tensor_copy(kd4[:, t, j, :, :].rearrange("p g (u d) -> p g u d", u=2),
                                                  kv5[:, t, j, :, :].unsqueeze(2).broadcast_to([P, NSA_G, 2, HD]))
                    dve.wait_ge(E["hn_r"], 3)
                    for jj, j in enumerate((2, 4)):
                        for t in range(NT):
                            c = 4 * jj + 2 * t
                            i = nc.vector.tensor_tensor(kd4[:, t, 2 + jj, :, :].rearrange("p g (u d) -> p g u d", u=2),
                                                        kv5[:, t, j, :, :].unsqueeze(2)
                                                        .broadcast_to([P, NSA_G, 2, HD]),
                                                        hrs[:, c:c + 2].unsqueeze(2).unsqueeze(3)
                                                        .broadcast_to([P, NSA_G, 2, HD]), ALU.mult)
                    i.then_inc(E["kd_ready"], 1)
                    q0, m0 = NSA_H * HD, NSA_H * HD + 3 * NSA_H
                    for t, scratch in enumerate((LbF, PbF)):
                        nc.vector.tensor_tensor(scratch[:, 0:q0], z1[:, t, 0:q0], z1[:, t, 0:q0], ALU.mult)
                        i = nc.vector.tensor_tensor(scratch[:, q0:q0 + MEM_W], z1[:, t, m0:B_IN], z1[:, t, m0:B_IN],
                                                    ALU.mult)
                    link(i)
                    for t, scratch in enumerate((LbF, PbF)):
                        i = nc.vector.tensor_reduce(hss[:, 16 * t:16 * t + 16],
                                                    scratch.rearrange("p (a d) -> p a d", d=HD), AX_X, ALU.add)
                    i.then_inc(E["hn_sq"], 1)
                    evac_units(kv_units())
                    dve.wait_ge(E["tt_a"], (n["T"] + 1) // 2)
                    dve.wait_ge(E["tt_d"], n["T"] // 2)
                    for w in range(2):
                        for g in range(NSA_G):
                            src = cmpT[:, NSA_G * w + g, :].rearrange("p (c l e) -> p l c e", l=8, e=2)[:, :, :, 0]
                            for half in range(2):
                                pos = COLS[("cmp_pos_2", w)] + 8 * half
                                i = nc.vector.tensor_tensor(flat[:, w, 8 * half:8 * half + 8, g, :],
                                                            src[:, :, half:half + NCMP],
                                                            col[:, pos:pos + 8].unsqueeze(2)
                                                            .broadcast_to([P, 8, NCMP]), ALU.add)
                    i.then_inc(E["flat_ready"], 1)
                    for w in range(2):
                        dve.wait_ge(E["fhi"], w + 1)
                        nc.vector.tensor_tensor(flatR[1][w], flat[:, w].rearrange("p l g c -> p (l g c)"),
                                                flatR[0][w].bitcast(F32), ALU.subtract).then_inc(E["flo"], 1)
                    dve.wait_ge(E["hn_r"], 4)
                    for t in range(NT):
                        for c0, m, c in ((0, NSA_H, 0), (m0, MEM_H, NSA_H)):
                            qv = z1[:, t, c0:c0 + m * HD].rearrange("p (a d) -> p a d", d=HD)
                            i = nc.vector.scalar_tensor_tensor(qv, qv, HD ** -0.5,
                                                               hrs[:, 16 * t + c:16 * t + c + m].unsqueeze(2)
                                                               .broadcast_to([P, m, HD]), op0=ALU.mult, op1=ALU.mult)
                    i.then_inc(E["qn_ready"], 1)
                    link(nc.vector.memset(gel4, 0.0))
                    for w in range(2):
                        split_upto(FIRST[("cmp", w)] + 2 + RH)
                        dve.wait_ge(E["gel_t"], w + 1)
                        for j in range(2):
                            i = nc.vector.tensor_copy(gel4[:, w, j].rearrange("p g (r c) -> p g r c", r=4)[:, :, :, 0:NCMP],
                                                      PS[w][:, 256 + 32 * j:256 + 32 * j + 30]
                                                      .rearrange("p (g c) -> p g c", g=NSA_G)
                                                      .unsqueeze(2).broadcast_to([P, NSA_G, 4, NCMP]))
                    i.then_inc(E["rep_done"], 1)
                    dve.wait_ge(E["kc_mm"], 1)
                    link(nc.vector.tensor_copy(kvc, PS[2][:, 0:4 * HD].rearrange("p (a d) -> p a d", a=4)))
                    link(nc.vector.tensor_tensor(part[:, 0:P].rearrange("p (g d) -> p g d", g=NSA_G), kvc[:, 0:2, :],
                                                 kvc[:, 0:2, :], ALU.mult))
                    nc.vector.tensor_reduce(hss[:, 0:NSA_G], part[:, 0:P].rearrange("p (g d) -> p g d", g=NSA_G), AX_X,
                                            ALU.add).then_inc(E["hn_sq"], 1)
                    dve.wait_ge(E["hn_r"], 5)
                    nc.vector.tensor_tensor(kcd.rearrange("p g (u d) -> p g u d", u=2),
                                            kvc[:, 0:2, :].unsqueeze(2).broadcast_to([P, NSA_G, 2, HD]),
                                            hrs[:, 0:2].unsqueeze(2).unsqueeze(3).broadcast_to([P, NSA_G, 2, HD]),
                                            ALU.mult).then_inc(E["kcd_ready"], 1)
                    nc.vector.memset(kcT, 0.0)
                    link(nc.vector.memset(vdiag, 0.0))
                    for a in range(NSA_H):
                        rr = slice(32 * (a % 4), 32 * (a % 4) + 32)
                        i = nc.vector.tensor_copy(vdiag[rr, a, :], kvc[rr, NSA_G + a // HPG, :])
                    i.then_inc(E["vd_ready"], 1)
                    evac_units(query_units())
                    dve.wait_ge(E["kct_mm"], 1)
                    gcol = COLS[("k_gain_2", 0)]
                    for u in range(2):
                        rr = slice(HD * u, HD * u + HD)
                        i = nc.vector.tensor_scalar(kcT[rr, :, u, :], PS[3][rr, 0:32].rearrange("p (g c) -> p g c", g=NSA_G),
                                                    col[rr, gcol:gcol + 1], None, ALU.mult)
                    i.then_inc(E["kct_ready"], 1)
                    link(nc.vector.memset(PbF[:, 0:768], 0.0))
                    Lc = LbF[:, 0:768].rearrange("p (t a c) -> p t a c", t=NT, c=32)[:, :, :, 0:NCMP]
                    Lc2 = LbF[:, 0:768].rearrange("p (a c) -> p a c", c=32)[:, :, 0:NCMP]
                    dve.wait_ge(E["cs_done"], 1)
                    link(nc.vector.tensor_tensor(Lc, PS[0][:, 0:384].rearrange("p (t a c) -> p t a c", t=NT, c=16)
                                                 [:, :, :, 0:NCMP], Tcmp, ALU.add))
                    link(nc.vector.tensor_reduce(cmax, Lc2, AX_X, ALU.max))
                    nc.vector.tensor_tensor(Lc2, Lc2, cmax.unsqueeze(2).broadcast_to([P, NT * NSA_H, NCMP]),
                                            ALU.subtract).then_inc(E["cl_done"], 1)
                    dve.wait_ge(E["ce_done"], 1)
                    link(nc.vector.tensor_reduce(csum, PbF[:, 0:768].rearrange("p (a c) -> p a c", c=32)[:, :, 0:NCMP],
                                                 AX_X, ALU.add))
                    link(nc.vector.reciprocal(csum, csum))
                    cs = csum.rearrange("p (t a) -> p t a", t=NT)
                    link(nc.vector.tensor_tensor(cs, cs, cst[:, C_SEEN:C_SEEN + 2].unsqueeze(2)
                                                 .broadcast_to([P, NT, NSA_H]), ALU.mult))
                    dve.wait_ge(E["ct_done"], 1)
                    nc.vector.tensor_copy(PTbF[:, 0:384], PS[1][:, 0:384]).then_inc(E["cte_d"], 1)
                    dve.wait_ge(E["gat_done"], 1)
                    for a in range(0, NSA_H, 4):
                        outputs([HD * (a + j) for j in range(4)], n["O"],
                                csum.rearrange("p (t a) -> p a t", t=NT)[:, a:a + 4, :], (a, 0))
                        n["O"] += 4
                    attention(nsa_jobs(0) + nsa_jobs(1))
                    attention(mem_jobs(1))
                rest_T(2 if l == 0 else KD, xT, None, at=6 if l == 0 else 0)
                for p in range(FIRST[("w_out", l)], FIRST[("w_out", l)] + 4):
                    split_upto(p + 1 + RH)
                add_to_h(FIRST[("w_out", l)] + 4)
                scaled([xs], [h])
                rest_T(KD, xT, gains(("mlp_norm_2", l), KD))
                mlp(("ffn2", l), FF2 // 256, False)
                add_to_h(FIRST[("kv", 1)] if l == 0 else len(PIECES))

        @block.tensor
        def _(pe):
            n = dict(x=0, wide=0, T=0, J=0, B=0, X=0, F=0, G=0, O=0, xsr=0)

            def banks_free():
                for name, v in (("xlo", n["x"]), ("wide_a", n["wide"]), ("wide_d", n["wide"]), ("tt_a", (n["T"] + 1) // 2),
                                ("tt_d", n["T"] // 2), ("e_done", NT * n["J"]), ("pte_done", n["J"]),
                                ("o_evac", n["G"]), ("ix_r", n["X"]), ("sb_w", n["B"]), ("ff_hid", n["F"])):
                    if v:
                        pe.wait_ge(E[name], v)

            def slot(p):
                nk, w = PIECES[p][3], PIECES[p][5]
                return [r[:, p % RH, 0:nk * w].rearrange("p (k n) -> p k n", k=nk) for r in (w_hi, w_lo)]

            def by_tokens(out_, x, k, t, w, kk, c0, c1, start, stop):
                tok = slice(t * P, t * P + P)
                nc.tensor.matmul(out_, x[:, 0, k, tok], w[0][:, kk, c0:c1], start=start, stop=False)
                nc.tensor.matmul(out_, x[:, 0, k, tok], w[1][:, kk, c0:c1], start=False, stop=False)
                return nc.tensor.matmul(out_, x[:, 1, k, tok], w[0][:, kk, c0:c1], start=False, stop=stop)

            def by_weights(out_, x, k, w, kk, c0, start, stop):
                c = slice(c0, c0 + P)
                nc.tensor.matmul(out_, w[0][:, kk, c], x[:, 0, k, :], start=start, stop=False)
                nc.tensor.matmul(out_, w[0][:, kk, c], x[:, 1, k, :], start=False, stop=False)
                return nc.tensor.matmul(out_, w[1][:, kk, c], x[:, 0, k, :], start=False, stop=stop)

            def to_T(kn, src, wait_xs=True, again=False):
                banks_free()
                if again:
                    wait_xs = False
                if wait_xs:
                    for t in range(NT):
                        n["xsr"] += 1
                        pe.wait_ge(E["xs_ready"], n["xsr"])
                        for k in range(kn):
                            i = nc.tensor.transpose(PS[k // 2 % 4][:, (k % 2) * S + t * P:(k % 2) * S + t * P + P],
                                                    src[:, t, k * P:k * P + P], ident)
                            if t and (k % 2 or k == kn - 1):
                                i.then_inc(E["tr_done"], 1)
                    return
                for k in range(kn):
                    if k >= 8:
                        pe.wait_ge(E["xlo"], n["x"] + k - 7)
                    for t in range(NT):
                        i = nc.tensor.transpose(PS[k // 2 % 4][:, (k % 2) * S + t * P:(k % 2) * S + t * P + P],
                                                src[:, t, k * P:k * P + P], ident)
                    if k % 2 or k == kn - 1:
                        i.then_inc(E["tr_done"], 1)

            def x_block(k):
                pe.wait_ge(E["xlo"], n["x"] + k + 1)

            def units(list_):
                for u in list_:
                    U = n["T"]
                    if U >= 4:
                        pe.wait_ge(E["tt_a" if U % 2 == 0 else "tt_d"], (U - 4) // 2 + 1)
                    for j, (src, ws) in enumerate(u.srcs):
                        for t in range(NT):
                            i = nc.tensor.transpose(PS[U % 4][0:ws, j * S + t * P:j * S + t * P + P], src(t), ident)
                    i.then_inc(E["tt_done"], 1)
                    n["T"] += 1

            def units_moved():
                pe.wait_ge(E["tt_a"], (n["T"] + 1) // 2)
                pe.wait_ge(E["tt_d"], n["T"] // 2)

            def wide_product(stage, width, kn=KD, fresh=True):
                p = FIRST[stage]
                for c0 in range(0, width, 512):
                    w = min(512, width - c0)
                    b = 4 + 2 * (n["wide"] % 2)
                    if n["wide"] >= 2:
                        pe.wait_ge(E["wide_a"], n["wide"] - 1)
                        pe.wait_ge(E["wide_d"], n["wide"] - 1)
                    for k in range(kn):
                        nk = PIECES[p][3]
                        if k % nk == 0:
                            pe.wait_ge(E["lo_ready"], p + 1)
                        if c0 == 0 and fresh:
                            x_block(k)
                        ws = slot(p)
                        for t in range(NT):
                            i = by_tokens(PS[b + t][:, 0:w], xT, k, t, ws, k % nk, 0, w, k == 0, k == kn - 1)
                        if k % nk == nk - 1:
                            i.then_inc(E["piece_used"], 1)
                            p += 1
                    n["wide"] += 1
                if fresh:
                    n["x"] += kn

            def last_down(p, x, ks):
                ws = slot(p)
                for t in range(NT):
                    for c in range(2):
                        for kk, k in enumerate(ks):
                            i = by_tokens(PS[4 + 2 * t + c][:, :], x, k, t, ws, kk, 512 * c, 512 * c + 512,
                                          False, kk == 1)
                    i.then_inc(E["tok0_done" if t == 0 else "piece_used"], 1)

            def tall_product(stage, kn, x, base, counted=True, residual=False):
                p = FIRST[stage]
                for k in range(kn - 2 if residual else kn):
                    if k % 2 == 0:
                        pe.wait_ge(E["lo_ready"], p + 1)
                    if counted:
                        x_block(k)
                    ws = slot(p)
                    for t in range(NT):
                        for c in range(2):
                            i = by_tokens(PS[base + 2 * t + c][:, :], x, k, t, ws, k % 2, 512 * c, 512 * c + 512,
                                          k == 0, k == kn - 1)
                    if k % 2 == 1:
                        i.then_inc(E["piece_used"], 1)
                        p += 1
                if residual:
                    pe.wait_ge(E["lo_ready"], p + 1)
                    x_block(kn - 1)
                    last_down(p, x, (kn - 2, kn - 1))
                if counted:
                    n["x"] += kn

            def lora_product(stage, k0, kn, base, w):
                p = FIRST[stage]
                pe.wait_ge(E["lo_ready"], p + 1)
                ws = slot(p)
                for k in range(kn):
                    pe.wait_ge(E["xlo"], n["x"] + k0 + k + 1)
                    for t in range(NT):
                        for half in range(2):
                            i = by_tokens(PS[base + 2 * t + half][:, 0:w], hT, k0 + k, t, ws, k, w * half,
                                          w * half + w, k == 0, k == kn - 1)
                i.then_inc(E["piece_used"], 1)

            def mlp(stage, blocks, gated):
                p = FIRST[stage]
                per_up = 2 if gated else 1
                ups, downs = ffn_places(p, blocks, per_up)

                def up(c):
                    F = n["F"]
                    b = c % 2
                    if c >= 2:
                        pe.wait_ge(E["ff_hid"], F - 1)
                    for which in range(per_up):
                        q = ups[c] + which
                        pe.wait_ge(E["lo_ready"], q + 1)
                        ws = slot(q)
                        for j in range(2):
                            for k in range(KD):
                                if c == 0 and which == 0 and j == 0:
                                    x_block(max(k, 1))
                                i = by_weights(PS[2 * b + which][:, j * S:j * S + S], xT, k, ws, k, j * P, k == 0,
                                               k == KD - 1)
                        i.then_inc(E["piece_used"], 1)
                    n["F"] += 1

                def down(c, F):
                    q = downs[c]
                    pe.wait_ge(E["lo_ready"], q + 1)
                    pe.wait_ge(E["ff_lo"], F + 1)
                    if c == blocks - 1:
                        last_down(q, hT, (2 * (c % 2), 2 * (c % 2) + 1))
                        return
                    ws = slot(q)
                    for k in range(2):
                        for t in range(NT):
                            for half in range(2):
                                i = by_tokens(PS[4 + 2 * t + half][:, :], hT, 2 * (c % 2) + k, t, ws, k, 512 * half,
                                              512 * half + 512, c == 0 and k == 0, False)
                    i.then_inc(E["piece_used"], 1)

                F0 = n["F"]
                for c in range(blocks):
                    up(c)
                    if c:
                        down(c - 1, F0 + c - 1)
                down(blocks - 1, F0 + blocks - 1)
                n["x"] += KD

            def attention(jobs):
                J0 = n["J"]

                def scores(i):
                    job, J = jobs[i], J0 + i
                    if J >= 2:
                        pe.wait_ge(E["l_done" if job.causal else "e_done"], NT * (J - 1))
                    for t in (1, 0):
                        c, nk = spans(t, job.causal)
                        m = nc.tensor.matmul(PS[J % 2][:, c:c + nk], job.q[:, t * P:t * P + P], job.k[:, 0:nk],
                                             start=True, stop=True)
                    m.then_inc(E["s_done"], 1)

                def transposes(i):
                    J = J0 + i
                    pe.wait_ge(E["e_done"], NT * (J + 1))
                    if J >= 2:
                        pe.wait_ge(E["pte_done"], J - 1)
                    for j in range(3 if jobs[i].causal else 4):
                        m = nc.tensor.transpose(PS[2 + J % 2][:, j * P:j * P + P], Pb[:, J % 2, j * P:j * P + P], ident)
                    m.then_inc(E["pt_done"], 1)

                def values(i):
                    job, J = jobs[i], J0 + i
                    G = n["G"] + i // 4
                    if i % 4 == 0 and G >= 2:
                        pe.wait_ge(E["o_evac"], G - 1)
                    pe.wait_ge(E["pte_done"], J + 1)
                    o = PS[4 + G % 2][:, (i % 4) * 2 * HD:(i % 4) * 2 * HD + 2 * HD]
                    pt = PTb[:, J % 2, :]
                    if not job.causal:
                        for t in range(NT):
                            for kt in range(2):
                                m = nc.tensor.matmul(o[:, t * HD:t * HD + HD], pt[:, (2 * t + kt) * P:(2 * t + kt + 1) * P],
                                                     job.v(kt), start=kt == 0, stop=kt == 1)
                        m.then_inc(E["o_done"], 1)
                        return
                    nc.tensor.matmul(o[:, HD:2 * HD], pt[:, 0:P], job.v(0), start=True, stop=False)
                    nc.tensor.matmul(o[:, HD:2 * HD], pt[:, P:2 * P], job.v(1), start=False, stop=True)
                    m = nc.tensor.matmul(o[:, 0:HD], pt[:, 2 * P:3 * P], job.v(0), start=True, stop=True)
                    m.then_inc(E["o_done"], 1)

                scores(0)
                for i in range(len(jobs)):
                    if i + 1 < len(jobs):
                        scores(i + 1)
                    transposes(i)
                    if i:
                        values(i - 1)
                values(len(jobs) - 1)
                n["J"] += len(jobs)
                n["G"] += len(groups(jobs))

            def index_scores():
                for a in range(IDX_H):
                    X = n["X"]
                    if X >= 2:
                        pe.wait_ge(E["ix_r"], X - 1)
                    r = slice((a % 2) * 64, (a % 2) * 64 + 64)
                    for t in (1, 0):
                        c, nk = spans(t, True)
                        m = nc.tensor.matmul(PS[X % 2][:, c:c + nk], allT[r, B_IQ + a // 2, t * P:t * P + P],
                                             allT[r, B_IK, 0:nk], start=True, stop=True)
                    m.then_inc(E["ix_s"], 1)
                    n["X"] += 1

            def stick_breaking():
                B0 = n["B"]

                def z_of(i):
                    r = slice((i % 2) * 64, (i % 2) * 64 + 64)
                    bank = PS[SB_BANK[i]]
                    nc.tensor.matmul(bank[:, 0:S], allT[r, B_SK + i // 2, 0:P], allT[r, B_SQ + i // 2, :],
                                     start=True, stop=True)
                    nc.tensor.matmul(bank[:, S:384], allT[r, B_SK + i // 2, P:S], allT[r, B_SQ + i // 2, P:S],
                                     start=False, stop=True, skip_group_check=True).then_inc(E["sb_z"], 1)

                def suffix(i):
                    B = B0 + i
                    pe.wait_ge(E["sb_nl"], B + 1)
                    bank, nl = PS[SB_BANK[i]], sbN[i]
                    nc.tensor.matmul(bank[:, 0:S], tri, nl[:, 0:S], start=False, stop=True, skip_group_check=True)
                    nc.tensor.matmul(bank[:, P:S], ones, nl[:, S:384], start=False, stop=True, skip_group_check=True)
                    nc.tensor.matmul(bank[:, S:384], tri, nl[:, S:384], start=False, stop=True,
                                     skip_group_check=True).then_inc(E["sb_s"], 1)

                def values(i):
                    B = B0 + i
                    G = n["G"] + i // 4
                    if i % 4 == 0 and G >= 2:
                        pe.wait_ge(E["o_evac"], G - 1)
                    pe.wait_ge(E["sb_e"], B + 1)
                    o = PS[4 + G % 2][:, (i % 4) * 2 * HD:(i % 4) * 2 * HD + 2 * HD]
                    wt = sbL[i]
                    v = [proj[:, kt, O_SV + HD * i:O_SV + HD * i + HD] for kt in range(NT)]
                    nc.tensor.matmul(o[:, HD:2 * HD], wt[:, P:2 * P], v[0], start=True, stop=False)
                    nc.tensor.matmul(o[:, HD:2 * HD], wt[:, 2 * P:3 * P], v[1], start=False, stop=True)
                    nc.tensor.matmul(o[:, 0:HD], wt[:, 0:P], v[0], start=True, stop=True).then_inc(E["o_done"], 1)

                for i in range(SB_H):
                    z_of(i)
                for i in range(SB_H):
                    suffix(i)
                for i in range(SB_H):
                    values(i)
                n["B"] += SB_H
                n["G"] += 2

            pe.wait_ge(E["onehot_in"], 32)
            nc.tensor.matmul(PS[4][0:DSA_H + 1, :], tables[0:BUCKETS + 1, 0:DSA_H + 1], onehot[0:BUCKETS + 1, 0, :],
                             start=True, stop=True)
            nc.tensor.matmul(PS[5][0:NSA_H, :], tables[0:BUCKETS + 1, DSA_H + 1:NROWS], onehot[0:BUCKETS + 1, 1, :],
                             start=True, stop=True).then_inc(E["tab_mm"], 1)
            pe.wait_ge(E["cst_in"], 32)
            for l in range(DEPTH):
                to_T(KD, xs)
                if l == 0:
                    pe.wait_ge(E["tab_ev"], 2)
                wide_product(("w_in", l), D_IN)
                pe.wait_ge(E["wide_a"], n["wide"])
                pe.wait_ge(E["wide_d"], n["wide"])
                banks_free()
                if l == 0:
                    pe.wait_ge(E["toep_in"], 16 * (DSA_H + 1))
                    for j in range(3):
                        nc.tensor.matmul(PS[j][:, :], flip, Tdsa[:, 2 * j:2 * j + 2, :], start=True, stop=True
                                         ).then_inc(E["flipped"], 1)
                    pe.wait_ge(E["toep_ready"], 3)
                pe.wait_ge(E["dup_ready"], l + 1)
                units(proj_units())
                to_T(5, lora)
                lora_product(("uq", l), 0, 3, 4, 3 * QK)
                pe.wait_ge(E["xlo"], n["x"] + 5)
                lora_product(("ukv", l), 3, 2, 0, 384)
                n["x"] += 5
                units_moved()
                pe.wait_ge(E["uq_a"], l + 1)
                pe.wait_ge(E["ukv_a"], l + 1)
                pe.wait_ge(E["ukv_d"], l + 1)
                banks_free()
                units(cat_units())
                units_moved()
                index_scores()
                banks_free()
                stick_breaking()
                banks_free()
                attention(mla_jobs() + dsa_jobs())
                pe.wait_ge(E["o_evac"], n["G"])
                to_T(KD, xs, wait_xs=False)
                tall_product(("w_o", l), KD, xT, 4, residual=True)
                to_T(KD, xs)
                mlp(("ffn1", l), FF1 // 256, True)
                to_T(KD, xs)
                tall_product(("ple_gate", l), KD, xT, 4)
                pe.wait_ge(E["plo"], l + 1)
                tall_product(("ple_proj", l), 2, hT, 0, counted=False)

            pe.wait_ge(E["gn_in"], 16 * NSA_H)
            pe.wait_ge(E["h_ready"], 10 * DEPTH)
            for j in range(9):
                if j >= 4:
                    pe.wait_ge(E["fn_ev"], j - 3)
                a0, seg = 4 * (j // 3), j % 3
                nc.tensor.matmul(PS[j % 4][:, :], flip, Gnsa[:, a0:a0 + 4, P * seg:P * seg + P], start=True, stop=True
                                 ).then_inc(E["fn"], 1)
            pe.wait_ge(E["fn_ev"], 9)
            to_T(KD, xs)
            wide_product(("mem_kv", 0), 2 * MEM_W)
            wide_product(("mem_kv", 1), 2 * MEM_W, fresh=False)
            for l in range(DEPTH):
                to_T(KD, xs)
                if l == 0:
                    wide_product(("a_in", 0), A_IN)
                    pe.wait_ge(E["kn_ready"], 1)
                    units(mem_units())
                    pe.wait_ge(E["wide_a"], n["wide"])
                    pe.wait_ge(E["v_ready"], 1)
                    units(conv_units())
                    pe.wait_ge(E["qn_ready"], 1)
                    units(mem_query_units())
                    units_moved()
                    attention(mem_jobs(0))
                    pe.wait_ge(E["o_evac"], n["G"])
                    to_T(2, xs[:, :, CONV:D], wait_xs=False)
                else:
                    wide_product(("kv", 1), 6 * NSA_G * HD)
                    to_T(KD, xs, again=True)
                    wide_product(("b_in", 1), B_IN)
                    pe.wait_ge(E["kd_ready"], 1)
                    units(kv_units())
                    units_moved()
                    for w in range(2):
                        p = FIRST[("cmp", w)]
                        pe.wait_ge(E["flo"], w + 1)
                        pe.wait_ge(E["lo_ready"], p + 2)
                        o = PS[w][0:NSA_G * NCMP, 0:CMP_HID]
                        for lp in range(16):
                            wh, wl = [a[:, lp % 8, :] for a in slot(p + lp // 8)]
                            fh, fl = [flatR[hl][w][:, 30 * lp:30 * lp + 30] for hl in range(2)]
                            nc.tensor.matmul(o, fh, wh, start=lp == 0, stop=False)
                            nc.tensor.matmul(o, fh, wl, start=False, stop=False)
                            i = nc.tensor.matmul(o, fl, wh, start=False, stop=lp == 15)
                            if lp % 8 == 7:
                                i.then_inc(E["piece_used"], 1)
                    for w in range(2):
                        pe.wait_ge(E["gel_done"], w + 1)
                        for j in range(2):
                            c = 256 + 32 * j
                            i = nc.tensor.transpose(PS[w][:, c:c + 30], act_hid[0:30, w, P * j:P * j + P],
                                                    ident[0:30, 0:30])
                        i.then_inc(E["gel_t"], 1)
                    pe.wait_ge(E["w2_in"], 16)
                    pe.wait_ge(E["rep_done"], 1)
                    for w in range(2):
                        for g in range(NSA_G):
                            for j in range(2):
                                i = nc.tensor.matmul(PS[2][:, (2 * w + g) * HD:(2 * w + g + 1) * HD], gel4[:, w, j, g, :],
                                                     w2[:, w, j, :], start=j == 0, stop=j == 1)
                    i.then_inc(E["kc_mm"], 1)
                    pe.wait_ge(E["kcd_ready"], 1)
                    banks_free()
                    pe.wait_ge(E["qn_ready"], 2)
                    units(query_units())
                    units_moved()
                    for g in range(NSA_G):
                        i = nc.tensor.transpose(PS[3][:, 16 * g:16 * g + 16], kcd[0:16, g, :], ident[0:16, 0:16])
                    i.then_inc(E["kct_mm"], 1)
                    pe.wait_ge(E["kct_ready"], 1)
                    for t in range(NT):
                        for a in range(0, NSA_H, 2):
                            c = (t * NSA_H + a) * 16
                            i = nc.tensor.matmul(PS[0][:, c:c + 32], q8[:, a // 2, t * P:t * P + P],
                                                 kcT[:, a // HPG, :, :], start=True, stop=True)
                    i.then_inc(E["cs_done"], 1)
                    pe.wait_ge(E["ce_done"], 1)
                    for t in range(NT):
                        for a in range(3):
                            c = t * 384 + a * P
                            i = nc.tensor.transpose(PS[1 + t][:, a * P:a * P + P], PbF[:, c:c + P], ident)
                        i.then_inc(E["ct_done"], 1)
                    pe.wait_ge(E["cte_d"], 1)
                    pe.wait_ge(E["cte_a"], 1)
                    pe.wait_ge(E["vd_ready"], 1)
                    for a in range(0, NSA_H, 4):
                        G = n["G"] + a // 4
                        pe.wait_ge(E["o_evac"], G - 1)
                        o = PS[4 + G % 2][:, :].rearrange("p (a t d) -> p a t d", a=4, t=NT)
                        for t in range(NT):
                            c = t * 384 + (a // 4) * P
                            i = nc.tensor.matmul(o[:, :, t, :], PTbF[:, c:c + P], vdiag[:, a:a + 4, :],
                                                 start=True, stop=True)
                        i.then_inc(E["o_done"], 4)
                    n["G"] += 3
                    n["O"] += NSA_H
                    attention(nsa_jobs(0) + nsa_jobs(1))
                    banks_free()
                    attention(mem_jobs(1))
                    pe.wait_ge(E["o_evac"], n["G"])
                    to_T(KD, xs, wait_xs=False)
                if l == 0:
                    n["x"] += 6
                    pe.wait_ge(E["xlo"], n["x"])
                    n["x"] -= 6
                tall_product(("w_out", l), KD, xT, 4, residual=True)
                to_T(KD, xs)
                mlp(("ffn2", l), FF2 // 256, False)


_OUT = (1, S, D)
_WEIGHTS = ["w_in", "mla_w_uq", "mla_w_ukv", "w_o", "w_gate", "w_up", "w_down", "w_ple_gate", "w_ple_proj",
            "mem_w_kv_2", "a_w_in_2", "b_w_in_2", "w_kv_shared_2", "cmp_w1_2", "w_out_2", "w_up_2", "w_down_2"]


def kernel(**inputs):
    import numpy as _np
    import concourse.bacc as _bacc
    from concourse import mybir as _mybir
    from concourse.bass_utils import run_bass_kernel_spmd as _run

    nc = _bacc.Bacc("TRN2", target_bir_lowering=False, num_devices=1)
    arrays = {}

    def give(name, a):
        a = _np.ascontiguousarray(a)
        arrays[f"in_{name}_dram"] = a
        return nc.dram_tensor(f"in_{name}_dram", a.shape, _mybir.dt.from_np(a.dtype), kind="ExternalInput").ap()

    get = {k: _np.asarray(v) for k, v in inputs.items()}
    weights = {w: give(w, get[w] if get[w].ndim == 3 else get[w][None]) for w in _WEIGHTS}
    cols = _np.zeros((P, NCOLS), _np.float32)
    for (name, l), c in COLS.items():
        v = get[name] if l is None else get[name][0, l] if name == "a_conv_w_2" else get[name][l]
        if name in ("mem_k_gain_2", "mem_q_gain_2", "k_gain_2", "b_q_gain_2"):
            v = _np.concatenate([v, v])
        v = v.reshape(-1)
        cols[:, c:c + v.size // P] = v.reshape(-1, P).T
    tables = _np.zeros((BUCKETS + 1, NROWS), _np.float32)
    tables[BUCKETS, :] = NEG
    tables[:BUCKETS, 0:DSA_H] = get["rel_bias"]
    tables[:BUCKETS, DSA_H + 1:] = get["rel_bias_2"]
    out = nc.dram_tensor("out_0_dram", (S, D), F32, kind="ExternalOutput").ap()
    bass_two_blocks(nc, weights, give("x", get["x"][0]), give("p", get["p"][:, 0].transpose(0, 2, 1)),
                    give("cols", cols), give("consts", constants()), give("onehot", one_hot()),
                    give("tables", tables), give("final", get["final_norm"]),
                    give("mem", get["mem_2"][0]), give("w2", get["cmp_w2_2"]), out)
    r = _run(nc, [arrays], core_ids=[0])
    return r.results[0]["out_0_dram"].reshape(_OUT)
```
